# Optimizing a Trainium2 kernel written in Bass

```python
import jax, jax.numpy as jnp
from jax import lax
import numpy as np

D_MODEL = 2048
BATCH = 1
SEQ = 512
DEPTH = 2

H_A = 8
DH_A = 128
D_C = 256
H_I = 8
D_I = 64
INDEX_TOPK = 256
Q_BLOCK = 128
H_B = 4
DK_B = 128
DV_B = 256
RET_CHUNK = 128
RET_THETA = 10000.0
H_QK = 16
H_V = 32
DK_C = 128
DV_C = 128
CONV_K = 4
DN_CHUNK = 64

EPS = 1e-6
MIX_A = H_A * DH_A
MIX_B = H_B * DV_B
MIX_AB = MIX_A + MIX_B
MIX_C = H_V * DV_C
CONV_CH = 2 * H_QK * DK_C + MIX_C
AB_SPLITS = (MIX_A, D_C, H_I * D_I, D_I, H_I, H_B * DK_B, H_B * DK_B, MIX_B, MIX_AB)
AB_COLS = sum(AB_SPLITS)
DN_SPLITS = (CONV_CH, MIX_C, H_V, H_V)
DN_COLS = sum(DN_SPLITS)
N_EVEN = (DEPTH + 1) // 2
N_ODD = DEPTH // 2

kernel_name = "hybrid_dsa_retention_gdn"

def _split(a, sizes):
    return jnp.split(a, [int(v) for v in np.cumsum(sizes)[:-1]], axis=-1)

def rms_norm(x, g):
    x = x.astype(jnp.float32)
    return x * lax.rsqrt(jnp.mean(x * x, axis=-1, keepdims=True) + EPS) * g

def l2_norm(x):
    return x * lax.rsqrt(jnp.sum(x * x, axis=-1, keepdims=True) + EPS)

def dsa_attention(q, c, q_idx, k_idx, w_idx, kv_norm, w_uk, w_uv, q_norm, k_norm):
    B, S = c.shape[:2]
    topk = min(INDEX_TOPK, S // 4)
    c = rms_norm(c, kv_norm)
    k = rms_norm(c @ w_uk, k_norm)
    q = rms_norm(q, q_norm)
    w_idx = w_idx * (H_I ** -0.5 * D_I ** -0.5)
    nblk = S // Q_BLOCK

    def to_blocks(a):
        return a.reshape(B, nblk, Q_BLOCK, *a.shape[2:]).swapaxes(0, 1)

    gather = jax.vmap(lambda a, i: a[i])
    s_pos = jnp.arange(S)

    def block(args):
        qb, qib, wb, start = args
        t = start + jnp.arange(Q_BLOCK)
        causal = s_pos[None, :] <= t[:, None]
        iscore = jax.nn.relu(jnp.einsum('bqhd,bsd->bqhs', qib, k_idx))
        iscore = jnp.einsum('bqhs,bqh->bqs', iscore, wb)
        iscore = jnp.where(causal[None], iscore, -jnp.inf)
        _, idx = lax.top_k(iscore, topk)
        valid = idx <= t[None, :, None]
        k_sel = gather(k, idx)
        c_sel = gather(c, idx)
        logits = jnp.einsum('bqhd,bqkd->bqhk', qb, k_sel) * (DH_A ** -0.5)
        logits = jnp.where(valid[:, :, None, :], logits, -jnp.inf)
        p = jax.nn.softmax(logits, axis=-1)
        lat = jnp.einsum('bqhk,bqkc->bqhc', p, c_sel)
        return jnp.einsum('bqhc,hcd->bqhd', lat, w_uv)

    out = lax.map(block, (to_blocks(q), to_blocks(q_idx), to_blocks(w_idx),
                          jnp.arange(nblk) * Q_BLOCK))
    return out.swapaxes(0, 1).reshape(B, S, MIX_A)

def _rotary(x, cos, sin):
    x1, x2 = jnp.split(x, 2, axis=-1)
    return jnp.concatenate([x1 * cos - x2 * sin, x2 * cos + x1 * sin], axis=-1)

def retention(q, k, v, ret_norm):
    B, S = q.shape[:2]
    C = RET_CHUNK
    N = S // C
    pos = jnp.arange(S, dtype=jnp.float32)
    inv_freq = 1.0 / (RET_THETA ** jnp.linspace(0.0, 1.0, DK_B // 2, dtype=jnp.float32))
    ang = pos[:, None] * inv_freq[None, :]
    cos = jnp.cos(ang)[None, :, None, :]
    sin = jnp.sin(ang)[None, :, None, :]
    q = _rotary(q, cos, sin)
    k = _rotary(k, cos, sin) * (DK_B ** -0.5)
    log_gamma = jnp.log1p(-jnp.exp2(-5.0 - jnp.arange(H_B, dtype=jnp.float32)))

    def chunks(a):
        return a.reshape(B, N, C, H_B, a.shape[-1]).transpose(0, 3, 1, 2, 4)

    q, k, v = chunks(q), chunks(k), chunks(v.astype(jnp.float32))
    i = jnp.arange(C, dtype=jnp.float32)
    diff = i[:, None] - i[None, :]
    dmask = jnp.where(diff >= 0, jnp.exp(jnp.maximum(diff, 0.0)[None] * log_gamma[:, None, None]), 0.0)
    inner = jnp.einsum('bhncd,bhnjd->bhncj', q, k) * dmask[None, :, None]
    inner = jnp.einsum('bhncj,bhnje->bhnce', inner, v)
    lg = log_gamma[None, :, None, None, None]
    k_dec = k * jnp.exp((C - 1 - i)[:, None] * lg)
    kv = jnp.einsum('bhncd,bhnce->nbhde', k_dec, v)
    chunk_decay = jnp.exp(C * log_gamma)[None, :, None, None]

    def step(state, kv_n):
        return state * chunk_decay + kv_n, state

    _, prev = lax.scan(step, jnp.zeros((B, H_B, DK_B, DV_B), jnp.float32), kv)
    q_dec = q * jnp.exp((i + 1)[:, None] * lg)
    cross = jnp.einsum('bhncd,nbhde->bhnce', q_dec, prev)
    out = (inner + cross).transpose(0, 2, 3, 1, 4).reshape(B, S, H_B, DV_B)
    out = rms_norm(out, ret_norm.reshape(H_B, DV_B))
    return out.reshape(B, S, MIX_B)

def causal_conv(x, w):
    w = w.astype(x.dtype)
    return lax.conv_general_dilated(
        x, w[:, None, :], window_strides=(1,), padding=[(CONV_K - 1, 0)],
        dimension_numbers=('NWC', 'WIO', 'NWC'), feature_group_count=x.shape[-1])

def gated_delta_rule(q, k, v, beta, g):
    B, S = q.shape[:2]
    C = DN_CHUNK
    N = S // C

    def chunks(a):
        if a.ndim == 4:
            return a.reshape(B, N, C, H_V, a.shape[-1]).transpose(0, 3, 1, 2, 4)
        return a.reshape(B, N, C, H_V).transpose(0, 3, 1, 2)

    q = chunks(q) * (DK_C ** -0.5)
    k, v, beta = chunks(k), chunks(v), chunks(beta)
    g = jnp.cumsum(chunks(g), axis=-1)
    idx = jnp.arange(C)
    tri = idx[:, None] >= idx[None, :]
    strict = idx[:, None] > idx[None, :]
    decay = jnp.exp(jnp.where(tri, g[..., :, None] - g[..., None, :], -jnp.inf))
    k_beta = k * beta[..., None]
    v_beta = v * beta[..., None]
    lmat = jnp.where(strict, jnp.einsum('bhncd,bhnjd->bhncj', k_beta, k) * decay, 0.0)
    amat = lmat + jnp.eye(C, dtype=jnp.float32)
    u = lax.linalg.triangular_solve(amat, v_beta, left_side=True, lower=True, unit_diagonal=True)
    w = lax.linalg.triangular_solve(amat, k_beta * jnp.exp(g)[..., None],
                                    left_side=True, lower=True, unit_diagonal=True)
    attn = jnp.einsum('bhncd,bhnjd->bhncj', q, k) * decay
    g_last = g[..., -1]
    k_tail = k * jnp.exp(g_last[..., None] - g)[..., None]
    q_dec = q * jnp.exp(g)[..., None]
    xs = tuple(jnp.moveaxis(a, 2, 0) for a in (u, w, q_dec, k_tail, attn, jnp.exp(g_last)))

    def step(state, xs_n):
        u_n, w_n, qd_n, kt_n, at_n, gl_n = xs_n
        v_new = u_n - jnp.einsum('bhcd,bhde->bhce', w_n, state)
        o = jnp.einsum('bhcd,bhde->bhce', qd_n, state) + jnp.einsum('bhcj,bhje->bhce', at_n, v_new)
        state = state * gl_n[..., None, None] + jnp.einsum('bhcd,bhce->bhde', kt_n, v_new)
        return state, o

    _, o = lax.scan(step, jnp.zeros((B, H_V, DK_C, DV_C), jnp.float32), xs)
    return o.transpose(1, 0, 3, 2, 4).reshape(B, S, H_V, DV_C)

def setup_inputs(seed: int = 0) -> dict:
    key = jax.random.key(seed)
    ks = jax.random.split(key, 17)
    f32 = jnp.float32

    def normal(k, shape, scale):
        return scale * jax.random.normal(k, shape, f32)

    def gain(k, shape):
        return 1.0 + 0.1 * jax.random.normal(k, shape, f32)

    E, O = N_EVEN, N_ODD
    return {
        "x": normal(ks[0], (BATCH, SEQ, D_MODEL), 1.0),
        "ab_norm": gain(ks[1], (E, D_MODEL)),
        "ab_w_in": normal(ks[2], (E, D_MODEL, AB_COLS), D_MODEL ** -0.5),
        "ab_kv_norm": gain(ks[3], (E, D_C)),
        "ab_w_uk": normal(ks[4], (E, D_C, DH_A), D_C ** -0.5),
        "ab_w_uv": normal(ks[5], (E, H_A, D_C, DH_A), D_C ** -0.5),
        "ab_q_norm": gain(ks[6], (E, DH_A)),
        "ab_k_norm": gain(ks[7], (E, DH_A)),
        "ab_ret_norm": gain(ks[8], (E, MIX_B)),
        "ab_w_out": normal(ks[9], (E, MIX_AB, D_MODEL), MIX_AB ** -0.5),
        "dn_norm": gain(ks[10], (O, D_MODEL)),
        "dn_w_in": normal(ks[11], (O, D_MODEL, DN_COLS), D_MODEL ** -0.5),
        "dn_conv": normal(ks[12], (O, CONV_K, CONV_CH), CONV_K ** -0.5),
        "dn_a_log": jnp.log(jax.random.uniform(ks[13], (O, H_V), f32, 1.0, 16.0)),
        "dn_dt_bias": normal(ks[14], (O, H_V), 0.1),
        "dn_out_norm": gain(ks[15], (O, DV_C)),
        "dn_w_out": normal(ks[16], (O, MIX_C, D_MODEL), MIX_C ** -0.5),
    }

def reference(x, ab_norm, ab_w_in, ab_kv_norm, ab_w_uk, ab_w_uv, ab_q_norm, ab_k_norm,
              ab_ret_norm, ab_w_out, dn_norm, dn_w_in, dn_conv, dn_a_log, dn_dt_bias,
              dn_out_norm, dn_w_out):
    B, S, _ = x.shape
    h = x.astype(jnp.float32)
    for layer in range(DEPTH):
        j = layer // 2
        if layer % 2 == 0:
            proj = rms_norm(h, ab_norm[j]) @ ab_w_in[j]
            q_a, c, q_i, k_i, w_i, q_b, k_b, v_b, gate = _split(proj, AB_SPLITS)
            a_out = dsa_attention(q_a.reshape(B, S, H_A, DH_A), c,
                                  q_i.reshape(B, S, H_I, D_I), k_i, w_i,
                                  ab_kv_norm[j], ab_w_uk[j], ab_w_uv[j],
                                  ab_q_norm[j], ab_k_norm[j])
            b_out = retention(q_b.reshape(B, S, H_B, DK_B), k_b.reshape(B, S, H_B, DK_B),
                              v_b.reshape(B, S, H_B, DV_B), ab_ret_norm[j])
            y = jnp.concatenate([a_out, b_out], axis=-1) * jax.nn.silu(gate)
            h = h + y @ ab_w_out[j]
        else:
            proj = rms_norm(h, dn_norm[j]) @ dn_w_in[j]
            qkv, z, b_log, a_in = _split(proj, DN_SPLITS)
            qkv = jax.nn.silu(causal_conv(qkv, dn_conv[j]))
            q, k, v = _split(qkv, (H_QK * DK_C, H_QK * DK_C, MIX_C))
            q = jnp.repeat(l2_norm(q.reshape(B, S, H_QK, DK_C)), H_V // H_QK, axis=2)
            k = jnp.repeat(l2_norm(k.reshape(B, S, H_QK, DK_C)), H_V // H_QK, axis=2)
            v = v.reshape(B, S, H_V, DV_C)
            beta = jax.nn.sigmoid(b_log)
            g = -jnp.exp(dn_a_log[j].astype(jnp.float32)) * jax.nn.softplus(a_in + dn_dt_bias[j])
            o = gated_delta_rule(q, k, v, beta, g)
            o = rms_norm(o, dn_out_norm[j]) * jax.nn.silu(z.reshape(B, S, H_V, DV_C))
            h = h + o.reshape(B, S, MIX_C) @ dn_w_out[j]
    return h.astype(x.dtype)


_drawn_inputs = setup_inputs


def setup_inputs(seed=0):
    import zlib

    import numpy as np

    out = dict(_drawn_inputs(seed))
    spreads = {}
    factors = {'ab_kv_norm': 4.891,
     'ab_q_norm': 6.963,
     'ab_k_norm': 6.698,
     'dn_dt_bias': 8.0,
     'ab_ret_norm': 3.038,
     'dn_out_norm': 2.931}
    for name, (base, spread) in spreads.items():
        noise = np.random.default_rng([zlib.crc32(name.encode()), seed]).standard_normal(out[name].shape)
        drawn = base * np.exp(spread * noise) if base else spread * noise
        out[name] = __import__('jax').numpy.asarray(drawn.astype(out[name].dtype))
    for name, factor in factors.items():
        out[name] = (out[name] * factor).astype(out[name].dtype)
    return out
```

```python
import math
from contextlib import ExitStack

import numpy as np

import concourse.bass as bass
from concourse import mybir

F32, F32R = mybir.dt.float32, mybir.dt.float32r
ALU, ACT = mybir.AluOpType, mybir.ActivationFunctionType
ds, ts = bass.ds, bass.ts

P = 128
SEQ, DM = 512, 2048
NT = SEQ // P
KT = DM // P
H_A, D_C, H_I, D_I, TOPK = 8, 256, 8, 64, 128
H_B, DK_B, DV_B = 4, 128, 256
H_QK, H_V = 16, 32
EPS = 1e-6
CH = 2048

C_QA = 0
C_C = C_QA + H_A * P
C_QI = C_C + D_C
C_KI = C_QI + H_I * D_I
C_W = C_KI + D_I
C_QKVB = C_W + H_I
C_GATE = C_QKVB + 2 * H_B * DK_B + H_B * DV_B
C_K1 = H_QK * P
C_V1 = 2 * H_QK * P
C_Z1 = C_V1 + H_V * P
C_BA = C_Z1 + H_V * P

N_KI, N_QI, N_QKVB = 2, 3, 7
N_HEADS = N_QKVB + 16
N_OUT0 = N_HEADS + 24
N_BA = N_OUT0 + 16
N_FIRST = N_BA + 1
N_GROUPS = N_FIRST + 4
N_OUT1A = N_GROUPS + 6 * (H_QK - 1) + 2
N_OUT1B = N_OUT1A + 16
N_END = N_OUT1B + 16

HIDE = -1.0e30
TAKEN = -3.0e38
LEVELS = (2, 4, 8, 16, 32, 64)

_K = {}
_n = 0
for _name, _w in (("ident", P), ("ones", P), ("hide_low", P), ("tri_up", P), ("cos", NT * 64),
                  ("sin", NT * 64), ("ret_in", H_B), ("ret_kd", H_B), ("ret_ms", H_B),
                  ("ret_out", H_B), ("ret_cd", H_B)):
    _K[_name] = (_n, _w)
    _n += _w
K0_COLS = _n
_K1 = {}
_n = 0
for _name, _w in (("hide_up", P), ("pair_up", P), ("levels", P * len(LEVELS))):
    _K1[_name] = (_n, _w)
    _n += _w
K1_COLS = _n


def constant_tables():
    i = np.arange(P)
    k0 = np.zeros((P, K0_COLS), np.float32)
    k1 = np.zeros((P, K1_COLS), np.float32)

    def put(name, value):
        table, where = (k0, _K) if name in _K else (k1, _K1)
        a, w = where[name]
        table[:, a:a + w] = value

    put("ident", np.eye(P))
    put("ones", 1.0)
    put("hide_low", np.where(i[None, :] <= i[:, None], 0.0, HIDE))
    put("tri_up", i[None, :] >= i[:, None])
    pos = np.arange(SEQ, dtype=np.float32)
    inv = (1.0 / (np.float32(10000.0) ** np.linspace(0, 1, 64, dtype=np.float32))).astype(np.float32)
    ang = (pos[:, None] * inv[None, :]).astype(np.float32)
    for name, f in (("cos", np.cos), ("sin", np.sin)):
        put(name, f(ang).reshape(NT, P, 64).transpose(1, 0, 2).reshape(P, NT * 64))
    lg = np.log1p(-np.exp2(-5.0 - np.arange(H_B)))[None, :]
    col = i[:, None].astype(np.float64)
    put("ret_in", DK_B ** -0.5 * np.exp(-(col + 1) * lg))
    put("ret_kd", DK_B ** -0.5 * np.exp((P - 1 - col) * lg))
    put("ret_ms", np.exp(2 * (col + 1) * lg) / DV_B)
    put("ret_out", np.exp((col + 1) * lg))
    put("ret_cd", np.exp(P * lg) + 0 * col)
    put("hide_up", np.where(i[None, :] >= i[:, None], 0.0, HIDE))
    put("pair_up", (i[None, :] // 2 == i[:, None] // 2) & (i[None, :] > i[:, None]))
    a, _ = _K1["levels"]
    for n, b in enumerate(LEVELS):
        row, c = i[:, None] // b, i[None, :] // b
        k1[:, a + n * P:a + (n + 1) * P] = (row % 2 == 1) & (c == row - 1)
    return k0, k1


_V = {"ab_norm": (0, 16), "dn_norm": (16, 16), "ab_kv_norm": (32, 2), "ab_q_norm": (34, 1),
      "ab_k_norm": (35, 1), "ab_ret_norm": (36, 8), "dn_out_norm": (44, 1)}
V_ROWS = 45


def build(nc, A):
    ctx = ExitStack()
    with ctx:
        def sb(name, shape, dt=F32):
            return ctx.enter_context(nc.sbuf_tensor(name, shape, dt))

        sems = {}

        def sem(name):
            if name not in sems:
                sems[name] = ctx.enter_context(nc.semaphore(name))
            return sems[name]

        def scratch(name, shape):
            return nc.dram_tensor(name, shape, F32).ap()

        x_hi = sb("x_hi", [P, KT, SEQ], F32R)
        x_lo = sb("x_lo", [P, KT, SEQ], F32R)
        w_raw = sb("w_raw", [P, 2, CH])
        w_hi = sb("w_hi", [P, 2, CH], F32R)
        w_lo = sb("w_lo", [P, 2, CH], F32R)
        pool_cols = 24400
        pool = sb("pool", [P, pool_cols])
        bank = [ctx.enter_context(nc.psum_tensor(f"bank{i}", [P, 512], F32)) for i in range(8)]

        def region(start):
            at = [start]

            def take(*shape):
                n = int(np.prod(shape))
                a = pool[:, at[0]:at[0] + n]
                at[0] += n
                assert at[0] <= pool_cols, at[0]
                if len(shape) == 2:
                    a = a.rearrange("p (a b) -> p a b", a=shape[0])
                elif len(shape) == 3:
                    a = a.rearrange("p (a b c) -> p a b c", a=shape[0], b=shape[1])
                return a
            return take, at

        take, at = region(0)
        k0 = take(K0_COLS)
        vec = take(V_ROWS)
        kq_gain = take(1)
        eps_col, ln_col, one_col = take(1), take(1), take(1)
        taps = take(256)
        stat = take(16)
        rows_in = take(P)
        shared_end = at[0]

        def const(name):
            a, w = _K[name]
            return k0[:, a:a + w]

        ident, ones = const("ident"), const("ones")

        def vcol(name, j=0):
            a = _V[name][0] + j
            return vec[:, a:a + 1]

        take, _ = region(shared_end)
        rows = take(NT, DM)
        square_out = take(DM)
        take, _ = region(shared_end + NT * DM)
        y_stage = take(KT, SEQ)
        resid = take(2, NT, 512)

        take, at = region(shared_end)
        qkvb = take(NT, 2048)
        l0_start = at[0]
        bias = take(1280)
        c_n = take(NT, D_C)
        key_t = take(SEQ)
        after_keep = at[0]
        ki_t = take(SEQ)
        wi_t = take(SEQ)
        wi_n = take(NT, H_I)
        qi_t = take(2, SEQ)
        relu_s = take(2, 1152)
        top8 = take(3, 8)
        c_t = take(2, SEQ)
        k_n = take(NT, P)
        w_uk = take(2, P)
        take, at = region(after_keep)
        q_t = take(SEQ)
        q_sq = take(SEQ)
        prob = take(1280)
        prob_t = take(1280)
        lat_t = take(2, SEQ)
        w_uv = take(2, 2, P)
        rot = take(2, NT, P)
        rot_tmp = take(NT, 64)
        rot_t = take(2, SEQ)
        k_dec = take(NT, P)
        ret_s = take(3, DV_B)
        ret_n = take(NT, DV_B)
        gate = take(4, SEQ)
        soft = take(24)
        ret_c = take(5)
        inner_t = rot_t[:, 1, :]

        off = [0, 128, 384, 768]
        wid = [128, 256, 384, 512]
        toff = [0, 512, 896, 1152]

        take, at = region(shared_end)
        cs = take(4, SEQ)
        zs = take(2, SEQ)
        sq = take(2, SEQ)
        rs = take(2, SEQ)
        qn, kn = take(SEQ), take(SEQ)
        k_rows = take(NT, P)
        g_row = take(2, SEQ)
        dec = take(2, SEQ)
        eg = take(2, SEQ)
        q_dec = take(2, SEQ)
        k_tail = take(2, NT, P)
        attn_t = take(2, SEQ)
        f_up = take(2, SEQ)
        inv_p = take(2, SEQ)
        inv_t = take(2, SEQ)
        z_m = take(2, SEQ)
        v_n = take(2, NT, P)
        r_n = take(2, P)
        v_new = take(2, P)
        state = take(2, P)
        o_n = take(2, SEQ)
        y_out = take(2, SEQ)
        o_stat = take(2, 2, NT)
        k1 = take(K1_COLS)
        gate_tab = take(5, NT, H_V)
        gt = take(5, NT, 2)
        take, at = region(shared_end + NT * DM)
        ba_t = take(SEQ)
        a_t = take(SEQ)
        sp_1, sp_2, sp_3 = take(SEQ), take(SEQ), take(SEQ)
        head_cols = take(4)
        g_n = take(NT, H_V)

        def k1c(name):
            a, w = _K1[name]
            return k1[:, a:a + w]

        def tiled(ap, n=NT):
            return ap.rearrange("p (o c) -> p o c", o=1).broadcast_to([P, n, P])

        def by_tile(ap):
            return ap.rearrange("p (t c) -> p t c", t=NT)

        def spread(cols, w=P):
            n = cols.shape[1]
            return cols.rearrange("p (t o) -> p t o", o=1).broadcast_to([P, n, w])

        y0_rows = scratch("y0", (KT * P, SEQ))
        y1_rows = scratch("y1", (H_V * P, SEQ))
        y0 = y0_rows.rearrange("(k p) s -> k p s", p=P)
        y1 = y1_rows.rearrange("(k p) s -> k p s", p=P)
        _a = _K["ret_in"][0]
        ret_tab = k0[:, _a:_a + 5 * H_B].rearrange("p (k h) -> p k h", h=H_B)
        h_mid = scratch("h_mid", (SEQ, DM))
        g_rows = scratch("g_rows", (H_V, SEQ))

        class Chunk:

            def __init__(self, base, i=0, per=0):
                assert per % 2 == 0 or isinstance(i, int)
                if isinstance(i, int):
                    base, i, per = base + per * i, 0, 0
                self.base, self.i, self.per = base, i, per
                self.slot = base % 2

            def count(self, d=0):
                return self.base + d if self.per == 0 else self.i * self.per + (self.base + d)

            def loads(self):
                h = self.base // 2 + 1
                return 16 * h if self.per == 0 else self.i * (8 * self.per) + 16 * h

            def plus(self, d):
                return Chunk(self.base + d, self.i, self.per)

        def load_chunk(sp, c, src, cols=CH, kts=KT):
            if c.base >= 2:
                sp.wait_ge(sem("lo_ready"), c.count(-1))
            w = cols // kts
            dst = w_raw[:, c.slot, 0:cols].rearrange("p (k n) -> p k n", n=w)
            sp.dma_start(dst, src.rearrange("(k p) n -> p k n", p=P)).then_inc(
                sem(f"raw_loaded{c.slot}"), 16)

        def split_hi(act, c, cols=CH):
            act.wait_ge(sem(f"raw_loaded{c.slot}"), c.loads())
            if c.base >= 2:
                act.wait_ge(sem("chunk_done"), c.count(-1))
            act.activation(w_hi[:, c.slot, 0:cols], w_raw[:, c.slot, 0:cols], ACT.Copy).then_inc(
                sem("hi_ready"), 1)

        def split_lo(dve, c, cols=CH):
            dve.wait_ge(sem("hi_ready"), c.count(1))
            dve.tensor_tensor(w_lo[:, c.slot, 0:cols], w_raw[:, c.slot, 0:cols],
                              w_hi[:, c.slot, 0:cols].bitcast(F32), ALU.subtract).then_inc(
                sem("lo_ready"), 1)

        def t_products(pe, c, k_from=0, k_to=KT, width=P, free=None):
            if k_from == 0:
                pe.wait_ge(sem("lo_ready"), c.count(1))
                if free is not None:
                    pe.wait_ge(*free)
            out = bank[c.slot][0:width, :]
            for k in range(k_from, k_to):
                wh = w_hi[:, c.slot, k * width:(k + 1) * width]
                wl = w_lo[:, c.slot, k * width:(k + 1) * width]
                pe.matmul(out, wh, x_hi[:, k, :], start=(k == 0), stop=False)
                pe.matmul(out, wh, x_lo[:, k, :], start=False, stop=False)
                m = pe.matmul(out, wl, x_hi[:, k, :], start=False, stop=(k == KT - 1))
            if k_to == KT:
                m.then_inc(sem("chunk_done"), 1)

        def n_products(pe, c, q, free=None):
            pe.wait_ge(sem("lo_ready"), c.count(1))
            for t in range(NT):
                if q == 0 and free is not None:
                    pe.wait_ge(*free(t))
                for k in range(4):
                    kt = 4 * q + k
                    xh, xl = x_hi[:, kt, ts(t, P)], x_lo[:, kt, ts(t, P)]
                    wh = w_hi[:, c.slot, k * 512:(k + 1) * 512]
                    wl = w_lo[:, c.slot, k * 512:(k + 1) * 512]
                    pe.matmul(bank[t][:, :], xh, wh, start=(kt == 0), stop=False)
                    pe.matmul(bank[t][:, :], xh, wl, start=False, stop=False)
                    m = pe.matmul(bank[t][:, :], xl, wh, start=False, stop=(kt == KT - 1))
            m.then_inc(sem("chunk_done"), 1)

        def passed(eng, name):
            eng.sem_inc(sem(name), 1)

        def rstd(act, out, ssq, scale, steps, count, bias=0.0):
            act.activation(out, ssq, ACT.Ln, scale=scale, bias=eps_col).then_inc(sem(steps), 1)
            act.wait_ge(sem(steps), count)
            return act.activation(out, out, ACT.Exp, scale=-0.5, bias=bias)

        def norm_stats_act(act, lay):
            for t in range(NT):
                if lay == 0:
                    act.wait_ge(sem(f"x_loaded{t}"), 16)
                elif t == 0:
                    act.wait_ge(sem("block_summed"), 16)
                if t:
                    act.wait_ge(sem("rows_ssq"), NT * lay + t)
                act.activation(square_out, rows[:, t, :], ACT.Square,
                               accum_out=stat[:, t:t + 1]).then_inc(sem("rows_ssq"), 1)
            act.wait_ge(sem("rows_ssq"), NT * lay + NT)
            rstd(act, stat[:, 4:8], stat[:, 0:4], 1.0 / DM, "ln_done", 3 * lay + 1).then_inc(
                sem("rows_rstd"), 1)

        def norm_turn_act(act, lay, gain):
            for k in range(KT):
                act.wait_ge(sem("rows_turned"), KT * lay + k + 1)
                act.activation(x_hi[:, k, :], bank[4 + k % 4][:, :], ACT.Copy,
                               scale=vcol(gain, k)).then_inc(sem("x_hi_ready"), 1)

        def norm_rows_dve(dve, lay):
            dve.wait_ge(sem("rows_rstd"), lay + 1)
            if lay == 1:
                dve.wait_ge(sem("h_mid_stored"), 64)
            for t in range(NT):
                dve.tensor_scalar(rows[:, t, :], rows[:, t, :], stat[:, 4 + t:5 + t], None,
                                  ALU.mult).then_inc(sem("rows_scaled"), 1)

        def norm_turn_dve(dve, lay, gain):
            for k in range(KT):
                dve.wait_ge(sem("x_hi_ready"), KT * lay + k + 1)
                dve.scalar_tensor_tensor(out=x_lo[:, k, :], in0=bank[4 + k % 4][:, :],
                                         scalar=vcol(gain, k), in1=x_hi[:, k, :].bitcast(F32),
                                         op0=ALU.mult, op1=ALU.subtract).then_inc(sem("x_lo_ready"), 1)

        def norm_pe(pe, lay):
            pe.wait_ge(sem("rows_scaled"), NT * lay + NT)
            for k in range(KT):
                if k >= 4:
                    pe.wait_ge(sem("x_lo_ready"), KT * lay + k - 3)
                for t in range(NT):
                    m = pe.transpose(bank[4 + k % 4][:, ts(t, P)], rows[:, t, ts(k, P)], ident)
                m.then_inc(sem("rows_turned"), 1)
            pe.wait_ge(sem("x_lo_ready"), KT * lay + KT)

        PHASE = {"out0": 0, "out1a": 1, "out1b": 2}
        OUTS = {"out0": (N_OUT0, y0, 0, A["ab_w_out"], A["x"]),
                "out1a": (N_OUT1A, y1, 0, A["dn_w_out"], h_mid),
                "out1b": (N_OUT1B, y1, KT, A["dn_w_out"], None)}

        def out_sync(sp, tag):
            base, _, first, w, _ = OUTS[tag]
            with sp.Fori(0, 4) as b:
                for q in range(4):
                    load_chunk(sp, Chunk(base + q, b, 4),
                               w[(first + 4 * q) * P:(first + 4 * q + 4) * P, ds(b * 512, 512)], kts=4)

        def out_pool(eng, tag):
            base, src, first, _, res = OUTS[tag]
            if tag == "out1b":
                eng.wait_ge(sem("y_lo_ready"), 8)
            for q in range(4):
                eng.dma_start(y_stage[:, 4 * q:4 * q + 4, :],
                              src[first + 4 * q:first + 4 * q + 4].rearrange("k p s -> p k s")).then_inc(
                    sem(f"y_loaded{q}"), 16)
            for b in range(4):
                blk = slice(b * 512, (b + 1) * 512)
                if res is not None:
                    if b >= 2:
                        eng.wait_ge(sem("block_summed"), 16 * PHASE[tag] + 4 * (b - 1))
                    eng.dma_start(resid[:, b % 2], res[:, blk].rearrange(
                        "(t p) n -> p t n", p=P)).then_inc(sem(f"resid_loaded{b % 2}"), 16)
                if tag == "out0" and b >= 1 or tag == "out1b":
                    d = b - 1 if tag == "out0" else b
                    store_block(eng, tag, d)
            if tag == "out0":
                store_block(eng, tag, 3)

        def store_block(eng, tag, b):
            dst, done = (h_mid, "h_mid_stored") if tag == "out0" else (A["out"], "out_stored")
            blk = slice(b * 512, (b + 1) * 512)
            eng.wait_ge(sem("block_summed"), 16 * PHASE[tag] + 4 * (b + 1))
            eng.dma_start(dst[:, blk].rearrange("(t p) n -> p t n", p=P),
                          rows[:, :, blk]).then_inc(sem(done), 16)

        def out_y_act(act, tag):
            act.wait_ge(sem("chunk_done"), OUTS[tag][0])
            for q in range(4):
                act.wait_ge(sem(f"y_loaded{q}"), 16 * PHASE[tag] + 16)
                act.activation(x_hi[:, 4 * q:4 * q + 4, :], y_stage[:, 4 * q:4 * q + 4, :],
                               ACT.Copy).then_inc(sem("y_hi_ready"), 1)

        def out_act(act, tag):
            out_y_act(act, tag)
            for n in range(OUTS[tag][0] + 2, OUTS[tag][0] + 18):
                if n < N_END:
                    split_hi(act, Chunk(n), cols=cols_of(n))

        def out_dve(dve, tag):
            base, _, _, _, res = OUTS[tag]
            for q in range(4):
                dve.wait_ge(sem("y_hi_ready"), 4 * PHASE[tag] + q + 1)
                dve.tensor_tensor(x_lo[:, 4 * q:4 * q + 4, :], y_stage[:, 4 * q:4 * q + 4, :],
                                  x_hi[:, 4 * q:4 * q + 4, :].bitcast(F32),
                                  ALU.subtract).then_inc(sem("y_lo_ready"), 1)
            for b in range(4):
                for q in range(3):
                    if base + 4 * b + q + 2 < N_END:
                        split_lo(dve, Chunk(base + 4 * b + q + 2), cols=cols_of(base + 4 * b + q + 2))
                if res is not None:
                    dve.wait_ge(sem(f"resid_loaded{b % 2}"), 32 * PHASE[tag] + 16 * (b // 2 + 1))
                dve.wait_ge(sem("chunk_done"), base + 4 * b + 4)
                for t in range(NT):
                    r = rows[:, t, b * 512:(b + 1) * 512]
                    dve.tensor_tensor(r, bank[t][:, :], r if res is None else resid[:, b % 2, t, :],
                                      ALU.add).then_inc(sem("block_summed"), 1)
                if base + 4 * b + 5 < N_END:
                    split_lo(dve, Chunk(base + 4 * b + 5), cols=cols_of(base + 4 * b + 5))

        def out_pe(pe, tag):
            base = OUTS[tag][0]
            pe.wait_ge(sem("y_lo_ready"), 4 * PHASE[tag] + 4)
            for q in range(4):
                n_products(pe, Chunk(base + q), q)
            with pe.Fori(1, 4) as b:
                for q in range(4):
                    n_products(pe, Chunk(base + q, b, 4), q,
                               free=lambda t: (sem("block_summed"), b * 4 + (16 * PHASE[tag] + t - 3)))

        def cols_of(n):
            return {N_KI: KT * 72, N_BA: KT * 64}.get(n, CH)


        IDX_T = (1, 2, 3)
        ioff = {1: 0, 2: 256, 3: 640}

        def pre_pe(pe):
            pe.wait_ge(sem("small_loaded"), 16 * 11)
            pe.transpose(bank[0][:, 0:V_ROWS], rows_in[0:V_ROWS, :], ident[0:V_ROWS, 0:V_ROWS]).then_inc(
                sem("gains_turned"), 1)
            for j in range(2):
                m = pe.transpose(bank[1][:, ts(j, P)], y_stage[:, 8 + j, 0:P], ident)
            m.then_inc(sem("gains_turned"), 1)
            norm_pe(pe, 0)
            pe.wait_ge(sem("vec_ready"), 2)
            t_products(pe, Chunk(0))
            t_products(pe, Chunk(1))
            t_products(pe, Chunk(N_KI), width=72, free=(sem("l0_drained"), 1))
            pe.wait_ge(sem("c_raw"), 2)
            for t in range(NT):
                for j in range(2):
                    m = pe.transpose(bank[2 + t // 2][:, (t % 2) * D_C + j * P:(t % 2) * D_C + (j + 1) * P],
                                     c_t[:, j, ts(t, P)], ident)
            m.then_inc(sem("latent_steps"), 1)
            t_products(pe, Chunk(3), free=(sem("l0_drained"), 2))
            pe.wait_ge(sem("wi_raw"), 1)
            for t in range(NT):
                m = pe.transpose(bank[4][:, t * H_I:(t + 1) * H_I], wi_t[0:H_I, ts(t, P)], ident[0:H_I, 0:H_I])
            m.then_inc(sem("latent_steps"), 1)
            pe.wait_ge(sem("c_n_ready"), NT)
            for j in range(2):
                for t in range(NT):
                    m = pe.transpose(bank[2 + j][:, ts(t, P)], c_n[:, t, ts(j, P)], ident)
            m.then_inc(sem("latent_steps"), 1)

            def index_head(h):
                pe.wait_ge(sem("qi_ready"), h // 2 + 1)
                if h >= 1:
                    pe.wait_ge(sem("relu_ready"), 3 * h)
                r = slice(64 * (h % 2), 64 * (h % 2) + 64)
                for t in IDX_T:
                    m = pe.matmul(bank[4 + t][:, 0:wid[t]], qi_t[r, (h // 2) % 2, ts(t, P)],
                                  ki_t[r, 0:wid[t]], start=True, stop=True)
                m.then_inc(sem("index_done"), 1)

            pe.wait_ge(sem("ki_ready"), 2)
            t_products(pe, Chunk(4), 0, 8, free=(sem("l0_drained"), 3))
            index_head(0)
            t_products(pe, Chunk(4), 8, KT)
            index_head(1)
            pe.wait_ge(sem("ct_ready"), 2)
            pe.wait_ge(sem("wi_n_ready"), 1)
            for t in range(NT):
                for j in range(2):
                    m = pe.matmul(bank[4][:, ts(t, P)], c_t[:, j, ts(t, P)], w_uk[:, j, :],
                                  start=(j == 0), stop=(j == 1))
            m.then_inc(sem("latent_steps"), 1)
            t_products(pe, Chunk(5), 0, 8, free=(sem("l0_drained"), 4))
            index_head(2)
            t_products(pe, Chunk(5), 8, KT)
            index_head(3)
            pe.wait_ge(sem("k_n_ready"), NT)
            for t in range(NT):
                m = pe.transpose(bank[2][:, ts(t, P)], k_n[:, t, :], ident)
            m.then_inc(sem("latent_steps"), 1)
            t_products(pe, Chunk(6), 0, 8, free=(sem("l0_drained"), 5))
            index_head(4)
            t_products(pe, Chunk(6), 8, KT)
            for h in (5, 6, 7):
                index_head(h)
            pe.wait_ge(sem("key_ready"), 1)
            pe.wait_ge(sem("l0_drained"), 7)
            with pe.Fori(0, 4) as b:
                for q in range(4):
                    n_products(pe, Chunk(N_QKVB + q, b, 4), q,
                               free=lambda t: (sem("l0_drained"), b * 4 + (t + 4)))

        def pre_sync(sp):
            for t in range(NT):
                sp.dma_start(rows[:, t, :], A["x"][ts(t, P), :]).then_inc(sem(f"x_loaded{t}"), 16)
            for n in range(7):
                if n < 2:
                    load_chunk(sp, Chunk(n), A["ab_w_in"][:, C_C + n * P:C_C + (n + 1) * P])
                elif n == N_KI:
                    load_chunk(sp, Chunk(n), A["ab_w_in"][:, C_KI:C_KI + 72], cols=KT * 72)
                else:
                    a = C_QI + (n - N_QI) * P
                    load_chunk(sp, Chunk(n), A["ab_w_in"][:, a:a + P])
            with sp.Fori(0, 4) as b:
                for q in range(4):
                    load_chunk(sp, Chunk(N_QKVB + q, b, 4),
                               A["ab_w_in"][q * 512:(q + 1) * 512, ds(b * 512 + C_QKVB, 512)], kts=4)

        def pre_act(act):
            act.dma_start(k0, A["k0"]).then_inc(sem("small_loaded"), 16)
            for name, (a, n) in _V.items():
                act.dma_start(rows_in[a:a + n, :], A[name]).then_inc(sem("small_loaded"), 16)
            for j in range(2):
                act.dma_start(y_stage[:, 8 + j, 0:P], A["dn_conv"][ts(j, P), :]).then_inc(sem("small_loaded"), 16)
            act.dma_start(w_uk, A["ab_w_uk"].rearrange("(j p) d -> p j d", p=P)).then_inc(sem("small_loaded"), 16)
            act.wait_ge(sem("eps_ready"), 3)
            norm_stats_act(act, 0)
            act.wait_ge(sem("gains_turned"), 1)
            act.activation(vec, bank[0][:, 0:V_ROWS], ACT.Copy).then_inc(sem("vec_ready"), 1)
            act.wait_ge(sem("gains_turned"), 2)
            act.activation(taps, bank[1][:, 0:256], ACT.Copy).then_inc(sem("vec_ready"), 1)
            act.wait_ge(sem("vec_ready"), 2)
            split_hi(act, Chunk(0))
            split_hi(act, Chunk(1))
            norm_turn_act(act, 0, "ab_norm")

            def drain(n, out, part=slice(0, P), then=None, at=None):
                act.wait_ge(sem("chunk_done"), n + 1)
                return act.activation(out, bank[n % 2][part, :], ACT.Copy)

            def relu(h):
                act.wait_ge(sem("index_done"), h + 1)
                if h >= 2:
                    act.wait_ge(sem("score_added"), 3 * (h - 1))
                for t in IDX_T:
                    act.activation(relu_s[:, h % 2, ioff[t]:ioff[t] + wid[t]], bank[4 + t][:, 0:wid[t]],
                                   ACT.Relu).then_inc(sem("relu_ready"), 1)

            for n in (0, 1):
                split_hi(act, Chunk(n + 2), cols=cols_of(n + 2))
                m = drain(n, c_t[:, n, :])
                m.then_inc(sem("c_raw"), 1)
                act.wait_ge(sem("c_raw"), n + 1)
                act.sem_inc(sem("l0_drained"), 1)
            split_hi(act, Chunk(4))
            act.wait_ge(sem("chunk_done"), 3)
            for half in range(2):
                act.activation(ki_t[64 * half:64 * half + 64, :], bank[0][0:64, :], ACT.Copy).then_inc(
                    sem("ki_ready"), 1)
            act.activation(wi_t[0:H_I, :], bank[0][64:64 + H_I, :], ACT.Copy,
                           scale=H_I ** -0.5 * D_I ** -0.5).then_inc(sem("wi_raw"), 1)
            act.wait_ge(sem("wi_raw"), 1)
            act.wait_ge(sem("ki_ready"), 2)
            act.sem_inc(sem("l0_drained"), 1)
            act.wait_ge(sem("latent_steps"), 1)
            for t in range(NT):
                src = bank[2 + t // 2][:, (t % 2) * D_C:(t % 2 + 1) * D_C]
                act.activation(c_n[:, t, :], src, ACT.Square,
                               accum_out=stat[:, 8 + t:9 + t]).then_inc(sem("small_ssq"), 1)
            act.wait_ge(sem("small_ssq"), NT)
            rstd(act, stat[:, 12:16], stat[:, 8:12], 1.0 / D_C, "ln_done", 2).then_inc(sem("small_rstd"), 1)
            act.wait_ge(sem("small_rstd"), 1)
            for t in range(NT):
                act.activation(c_n[:, t, :], bank[2 + t // 2][:, (t % 2) * D_C:(t % 2 + 1) * D_C], ACT.Copy,
                               scale=stat[:, 12 + t:13 + t]).then_inc(sem("c_n_ready"), 1)

            def drain_qi(j):
                n = N_QI + j
                if j >= 2:
                    act.wait_ge(sem("index_done"), 2 * (j - 1))
                drain(n, qi_t[:, j % 2, :]).then_inc(sem("qi_ready"), 1)
                act.wait_ge(sem("qi_ready"), j + 1)
                act.sem_inc(sem("l0_drained"), 1)

            split_hi(act, Chunk(5))
            drain_qi(0)
            act.wait_ge(sem("latent_steps"), 2)
            act.activation(wi_n, bank[4][:, 0:NT * H_I].rearrange("p (t h) -> p t h", t=NT),
                           ACT.Copy).then_inc(sem("wi_n_ready"), 1)
            act.wait_ge(sem("latent_steps"), 3)
            for j in range(2):
                act.activation(c_t[:, j, :], bank[2 + j][:, :], ACT.Copy,
                               scale=vcol("ab_kv_norm", j)).then_inc(sem("ct_ready"), 1)
            relu(0)
            split_hi(act, Chunk(6))
            drain_qi(1)
            relu(1)
            act.wait_ge(sem("latent_steps"), 4)
            for t in range(NT):
                act.activation(k_n[:, t, :], bank[4][:, ts(t, P)], ACT.Square,
                               accum_out=stat[:, t:t + 1]).then_inc(sem("small_ssq"), 1)
            act.wait_ge(sem("small_ssq"), 2 * NT)
            rstd(act, stat[:, 4:8], stat[:, 0:4], 1.0 / P, "ln_done", 3).then_inc(sem("small_rstd"), 1)
            act.wait_ge(sem("small_rstd"), 2)
            for t in range(NT):
                act.activation(k_n[:, t, :], bank[4][:, ts(t, P)], ACT.Copy,
                               scale=stat[:, 4 + t:5 + t]).then_inc(sem("k_n_ready"), 1)
            relu(2)
            split_hi(act, Chunk(7))
            drain_qi(2)
            relu(3)
            act.wait_ge(sem("latent_steps"), 5)
            act.wait_ge(sem("kq_gain_ready"), 1)
            act.activation(key_t, bank[2][:, :], ACT.Copy, scale=kq_gain).then_inc(sem("key_ready"), 1)
            relu(4)
            split_hi(act, Chunk(8))
            drain_qi(3)
            for h in (5, 6, 7):
                relu(h)
            with act.Fori(0, 4) as b:
                for q in range(4):
                    c = Chunk(N_QKVB + q, b, 4)
                    if q == 3:
                        act.wait_ge(sem("chunk_done"), c.count(1))
                        for t in range(NT):
                            act.activation(qkvb[:, t, ds(b * 512, 512)], bank[t][:, :],
                                           ACT.Copy).then_inc(sem("l0_drained"), 1)
                    split_hi(act, c.plus(2))

        def pre_dve(dve):
            dve.memset(eps_col, EPS).then_inc(sem("eps_ready"), 1)
            dve.memset(one_col, 1.0).then_inc(sem("eps_ready"), 1)
            dve.memset(ln_col, -0.5 * math.log(P)).then_inc(sem("eps_ready"), 1)
            dve.wait_ge(sem("eps_ready"), 3)
            norm_rows_dve(dve, 0)
            split_lo(dve, Chunk(0))
            split_lo(dve, Chunk(1))
            dve.wait_ge(sem("vec_ready"), 2)
            dve.tensor_tensor(kq_gain, vcol("ab_q_norm"), vcol("ab_k_norm"), ALU.mult).then_inc(
                sem("kq_gain_ready"), 1)
            norm_turn_dve(dve, 0, "ab_norm")

            def add_scores(h):
                if h == 0:
                    dve.wait_ge(sem("wi_n_ready"), 1)
                for j, t in enumerate(IDX_T):
                    dve.wait_ge(sem("relu_ready"), 3 * h + j + 1)
                    r = relu_s[:, h % 2, ioff[t]:ioff[t] + wid[t]]
                    sc = bias[:, off[t]:off[t] + wid[t]]
                    w = wi_n[:, t, h:h + 1]
                    if h == 0:
                        dve.tensor_scalar(sc, r, w, None, ALU.mult).then_inc(sem("score_added"), 1)
                    else:
                        dve.wait_ge(sem("score_added"), 3 * (h - 1) + j + 1)
                        dve.scalar_tensor_tensor(out=sc, in0=r, scalar=w, in1=sc, op0=ALU.mult,
                                                 op1=ALU.add).then_inc(sem("score_added"), 1)

            for n in (2, 3, 4, 5):
                split_lo(dve, Chunk(n), cols=cols_of(n))
            add_scores(0)
            split_lo(dve, Chunk(6))
            add_scores(1)
            add_scores(2)
            split_lo(dve, Chunk(7))
            add_scores(3)
            add_scores(4)
            split_lo(dve, Chunk(8))
            for h in (5, 6, 7):
                add_scores(h)
            for j, t in enumerate(IDX_T):
                dve.wait_ge(sem("score_added"), 3 * 7 + j + 1)
                d = bias[:, off[t] + t * P:off[t] + (t + 1) * P]
                dve.tensor_tensor(d, d, const("hide_low"), ALU.add).then_inc(sem("ranked"), 1)
            dve.tensor_copy(bias[:, 0:P], const("hide_low")).then_inc(sem("bias_ready"), 1)
            with dve.Fori(0, 4) as b:
                for q in range(4):
                    for j, t in enumerate(IDX_T):
                        dve.wait_ge(sem("ranked"), b * 24 + (6 * q + j + 1))
                        passed(dve, "dve_passed")
                        dve.max(top8[:, j, :], bias[:, off[t]:off[t] + wid[t]]).then_inc(sem("ranked"), 1)
                    for j, t in enumerate(IDX_T):
                        dve.wait_ge(sem("ranked"), b * 24 + (6 * q + j + 4))
                        sc = bias[:, off[t]:off[t] + wid[t]]
                        passed(dve, "dve_passed")
                        dve.match_replace(sc, top8[:, j, :], sc, TAKEN).then_inc(sem("ranked"), 1)
                    split_lo(dve, Chunk(N_QKVB + q + 2, b, 4))
            assert TOPK == 16 * 8
            for j, t in enumerate(IDX_T):
                dve.wait_ge(sem("ranked"), 3 + 96)
                sc = bias[:, off[t]:off[t] + wid[t]]
                dve.tensor_scalar(sc, sc, -2.0e38, HIDE, ALU.is_gt, ALU.mult).then_inc(sem("bias_ready"), 1)
            dve.wait_ge(sem("bias_ready"), 4)

        def hc(i, k):
            return Chunk(N_HEADS + k, i, 6)

        def n(i, per, k):
            return per * i + k if isinstance(i, int) else i * per + k

        def earlier(eng, name, i, per):
            if not (isinstance(i, int) and i == 0):
                eng.wait_ge(sem(name), n(i, per, 0))

        def heads_sync(sp):
            heads_sync_one(sp, 0)
            with sp.Fori(1, 4) as i:
                heads_sync_one(sp, i)

        def heads_sync_one(sp, i):
            cols = [i * 256 + C_QA, i * 256 + C_GATE, i * 256 + C_QA + P, i * 256 + C_GATE + P,
                    i * 256 + C_GATE + 1024, i * 256 + C_GATE + 1024 + P]
            for k in range(6):
                load_chunk(sp, hc(i, k), A["ab_w_in"][:, ds(cols[k], P)])
                if k == 2:
                    earlier(sp, "uv_done", i, 2)
                    for e in range(2):
                        sp.dma_start(w_uv[:, e], A["ab_w_uv"][ds(i * 512 + e * 256, 256), :].rearrange(
                            "(j p) d -> p j d", p=P)).then_inc(sem(f"uv_loaded{e}"), 16)

        def heads_pe(pe):
            heads_pe_one(pe, 0)
            with pe.Fori(1, 4) as i:
                heads_pe_one(pe, i)

        def heads_pe_one(pe, i):
            def prod(k, a=0, b=KT):
                c = hc(i, k)
                t_products(pe, c, a, b, free=(sem("l0_drained"), c.count(-1)))

            def logits(e, ssq_bank):
                pe.wait_ge(sem("q_sq_ready"), n(i, 2, e + 1))
                for t in range(NT):
                    m = pe.matmul(bank[ssq_bank][:, t:t + 1], q_sq[:, ts(t, P)], ones[:, 0:1],
                                  start=True, stop=True)
                m.then_inc(sem("q_ssq_done"), 1)
                for t in range(NT):
                    m = pe.matmul(bank[4 + t][:, 0:wid[t]], q_t[:, ts(t, P)], key_t[:, 0:wid[t]],
                                  start=True, stop=True)
                m.then_inc(sem("logits_done"), 1)

            def turn_prob(e):
                pe.wait_ge(sem("prob_ready"), n(i, 8, 4 * e + 4))
                for s in range(NT):
                    for t in range(s, NT):
                        m = pe.transpose(bank[4 + s][:, ts(t, P)],
                                         prob[:, off[t] + s * P:off[t] + (s + 1) * P], ident)
                    m.then_inc(sem("prob_turned"), 1)

            def latent(e):
                pe.wait_ge(sem("prob_t_act"), n(i, 4, 2 * e + 2))
                pe.wait_ge(sem("prob_t_dve"), n(i, 4, 2 * e + 2))
                for j in range(2):
                    for s in range(NT):
                        w = SEQ - s * P
                        m = pe.matmul(bank[4 + j][:, s * P:SEQ], c_n[:, s, ts(j, P)],
                                      prob_t[:, toff[s]:toff[s] + w], start=(s == 0), stop=(s == NT - 1))
                    m.then_inc(sem("lat_done"), 1)

            def up(e, b):
                pe.wait_ge(sem("lat_ready"), n(i, 4, 2 * e + 2))
                pe.wait_ge(sem(f"uv_loaded{e}"), n(i, 16, 16))
                for j in range(2):
                    m = pe.matmul(bank[b][:, :], w_uv[:, e, j, :], lat_t[:, j, :], start=(j == 0),
                                  stop=(j == 1))
                m.then_inc(sem("uv_done"), 1)

            prod(0)
            pe.wait_ge(sem("rot_ready"), n(i, 2, 2))
            earlier(pe, "ret_n_ready", i, 4)
            for j in range(2):
                for t in range(NT):
                    m = pe.transpose(bank[2 + j][:, ts(t, P)], rot[:, j, t, :], ident)
                m.then_inc(sem("rot_turned"), 1)
            prod(1, 0, 8)
            earlier(pe, "y_made", i, 4)
            pe.wait_ge(sem("rot_t_ready"), n(i, 2, 2))
            logits(0, 3)
            for t in range(NT):
                m = pe.matmul(bank[2][:, ts(t, P)], rot_t[:, 1, ts(t, P)], rot_t[:, 0, ts(t, P)],
                              start=True, stop=True)
            m.then_inc(sem("inner_done"), 1)
            prod(1, 8, KT)
            prod(2, 0, 8)
            turn_prob(0)
            pe.wait_ge(sem("inner_ready"), n(i, 1, 1))
            pe.wait_ge(sem("q_scale_ready"), n(i, 2, 1))
            for t in range(3):
                o = bank[2 + t // 2][:, (t % 2) * DV_B:(t % 2 + 1) * DV_B]
                m = pe.matmul(o, k_dec[:, t, :], qkvb[:, t, ds(i * DV_B + 1024, DV_B)],
                              start=True, stop=True)
            m.then_inc(sem("kv_done"), 1)
            prod(2, 8, KT)
            latent(0)
            prod(3, 0, 8)
            pe.wait_ge(sem("ret_s_ready"), n(i, 3, 3))
            up(0, 3)
            logits(1, 2)
            prod(3, 8, KT)
            prod(4, 0, 8)
            turn_prob(1)
            pe.wait_ge(sem("q_scale_ready"), n(i, 2, 2))
            pe.wait_ge(sem("y_made"), n(i, 4, 1))
            for t in range(NT):
                o = bank[2 + t // 2][:, (t % 2) * DV_B:(t % 2 + 1) * DV_B]
                m = pe.matmul(o, inner_t[:, ts(t, P)], qkvb[:, t, ds(i * DV_B + 1024, DV_B)],
                              start=True, stop=(t == 0))
                if t:
                    m = pe.matmul(o, rot_t[:, 0, ts(t, P)], ret_s[:, t - 1, :], start=False, stop=True)
            m.then_inc(sem("ret_out_done"), 1)
            prod(4, 8, KT)
            latent(1)
            prod(5, 0, 8)
            up(1, 6)
            pe.wait_ge(sem("ret_n_ready"), n(i, 4, 4))
            for j in range(2):
                for t in range(NT):
                    m = pe.transpose(bank[4 + j][:, ts(t, P)], ret_n[:, t, ts(j, P)], ident)
                m.then_inc(sem("ret_turned"), 1)
            prod(5, 8, KT)

        def heads_act(act):
            heads_act_one(act, 0)
            with act.Fori(1, 4) as i:
                heads_act_one(act, i)

        def heads_act_one(act, i):
            def after(k, out, func):
                split_hi(act, hc(i, k + 2))
                act.wait_ge(sem("chunk_done"), hc(i, k).count(1))
                act.activation(out, bank[hc(i, k).slot][:, :], func).then_inc(sem("l0_drained"), 1)

            def after_query(e):
                if e == 0:
                    earlier(act, "logits_done", i, 2)
                else:
                    act.wait_ge(sem("logits_done"), n(i, 2, 1))
                after(2 * e, q_t, ACT.Copy)
                act.wait_ge(sem("l0_drained"), hc(i, 2 * e).count(1))
                act.activation(q_sq, q_t, ACT.Square).then_inc(sem("q_sq_ready"), 1)

            def scale(e, b):
                act.wait_ge(sem("q_ssq_done"), n(i, 2, e + 1))
                rstd(act, soft[:, 0:4], bank[b][:, 0:4], 1.0 / P, "head_ln_done", n(i, 3, e + 1),
                     bias=ln_col).then_inc(sem("q_scale_ready"), 1)

            def exps(e):
                act.wait_ge(sem("soft_bias_ready"), n(i, 2, e + 1))
                for t in range(NT):
                    p = prob[:, off[t]:off[t] + wid[t]]
                    act.activation(p, p, ACT.Exp, scale=soft[:, t:t + 1], bias=soft[:, 8 + t:9 + t],
                                   accum_out=soft[:, 12 + t:13 + t]).then_inc(sem("exp_done"), 1)

            def drain_prob_t(e):
                for s in range(2):
                    act.wait_ge(sem("prob_turned"), n(i, 8, 4 * e + s + 1))
                    act.activation(prob_t[:, toff[s]:toff[s] + SEQ - s * P], bank[4 + s][:, s * P:SEQ],
                                   ACT.Copy).then_inc(sem("prob_t_act"), 1)

            def drain_latent(e):
                for j in range(2):
                    act.wait_ge(sem("lat_done"), n(i, 4, 2 * e + j + 1))
                    act.activation(lat_t[:, j, :], bank[4 + j][:, :], ACT.Copy,
                                   scale=vcol("ab_kv_norm", j)).then_inc(sem("lat_ready"), 1)

            after_query(0)
            earlier(act, "ret_out_done", i, 1)
            for j in range(2):
                act.wait_ge(sem("rot_turned"), n(i, 2, j + 1))
                act.activation(rot_t[:, j, :], bank[2 + j][:, :], ACT.Copy).then_inc(sem("rot_t_ready"), 1)
            scale(0, 3)
            earlier(act, "y0_stored0", i, 16)
            after(1, gate[:, 0, :], ACT.Silu)
            exps(0)
            drain_prob_t(0)
            after_query(1)
            drain_latent(0)
            scale(1, 2)
            earlier(act, "y0_stored1", i, 16)
            after(3, gate[:, 1, :], ACT.Silu)
            exps(1)
            drain_prob_t(1)
            act.wait_ge(sem("ret_out_done"), n(i, 1, 1))
            earlier(act, "ret_turned", i, 2)
            for t in range(NT):
                act.activation(ret_n[:, t, :], bank[2 + t // 2][:, (t % 2) * DV_B:(t % 2 + 1) * DV_B],
                               ACT.Square, accum_out=stat[:, t:t + 1]).then_inc(sem("ret_ssq"), 1)
            earlier(act, "y0_stored2", i, 16)
            after(4, gate[:, 2, :], ACT.Silu)
            act.wait_ge(sem("ret_ms_ready"), n(i, 1, 1))
            rstd(act, stat[:, 4:8], stat[:, 4:8], 1.0, "head_ln_done", n(i, 3, 3)).then_inc(sem("ret_rstd"), 1)
            act.wait_ge(sem("ret_scale_ready"), n(i, 1, 1))
            for t in range(NT):
                act.activation(ret_n[:, t, :], bank[2 + t // 2][:, (t % 2) * DV_B:(t % 2 + 1) * DV_B],
                               ACT.Copy, scale=stat[:, 8 + t:9 + t]).then_inc(sem("ret_n_ready"), 1)
            drain_latent(1)
            earlier(act, "y0_stored3", i, 16)
            after(5, gate[:, 3, :], ACT.Silu)

        def heads_dve(dve):
            heads_dve_one(dve, 0)
            with dve.Fori(1, 4) as i:
                heads_dve_one(dve, i)

        def heads_dve_one(dve, i):
            def soft_max(e):
                dve.wait_ge(sem("logits_done"), n(i, 2, e + 1))
                dve.wait_ge(sem("prob_turned"), n(i, 8, 4 * e))
                passed(dve, "dve_passed")
                for t in range(NT):
                    w = wid[t]
                    dve.tensor_tensor_reduce(out=prob[:, off[t]:off[t] + w], in0=bank[4 + t][:, 0:w],
                                             in1=bias[:, off[t]:off[t] + w], scale=1.0, scalar=-3.0e38,
                                             op0=ALU.add, op1=ALU.max,
                                             accum_out=soft[:, 4 + t:5 + t]).then_inc(sem("max_done"), 1)
                dve.wait_ge(sem("max_done"), n(i, 8, 4 * e + 4))
                dve.wait_ge(sem("q_scale_ready"), n(i, 2, e + 1))
                dve.scalar_tensor_tensor(out=soft[:, 8:12], in0=soft[:, 4:8], scalar=-1.0,
                                         in1=soft[:, 0:4], op0=ALU.mult, op1=ALU.mult).then_inc(
                    sem("soft_bias_ready"), 1)

            def normalise(e):
                dve.wait_ge(sem("exp_done"), n(i, 8, 4 * e + 4))
                dve.reciprocal(soft[:, 16:20], soft[:, 12:16]).then_inc(sem("sum_inverted"), 1)
                dve.wait_ge(sem("sum_inverted"), n(i, 2, e + 1))
                for t in range(NT):
                    p = prob[:, off[t]:off[t] + wid[t]]
                    dve.tensor_scalar(p, p, soft[:, 16 + t:17 + t], None, ALU.mult).then_inc(
                        sem("prob_ready"), 1)

            def drain_prob_t(e):
                for s in (2, 3):
                    dve.wait_ge(sem("prob_turned"), n(i, 8, 4 * e + s + 1))
                    dve.tensor_copy(prob_t[:, toff[s]:toff[s] + SEQ - s * P],
                                    bank[4 + s][:, s * P:SEQ]).then_inc(sem("prob_t_dve"), 1)

            def gated(e, b):
                dve.wait_ge(sem("uv_done"), n(i, 2, e + 1))
                dve.wait_ge(sem("l0_drained"), hc(i, 2 * e + 1).count(1))
                dve.tensor_tensor(gate[:, e, :], bank[b][:, :], gate[:, e, :], ALU.mult).then_inc(
                    sem("y_made"), 1)

            dve.tensor_copy(ret_c, ret_tab[:, :, ds(i, 1)].rearrange("p a b -> p (a b)")).then_inc(
                sem("ret_c_ready"), 1)
            dve.wait_ge(sem("ret_c_ready"), n(i, 1, 1))
            dve.wait_ge(sem("rot_ready"), n(i, 2, 2))
            earlier(dve, "kv_done", i, 1)
            dve.tensor_scalar(k_dec, rot[:, 1], ret_c[:, 1:2], None, ALU.mult).then_inc(
                sem("k_dec_ready"), 1)
            split_lo(dve, hc(i, 2))
            soft_max(0)
            dve.wait_ge(sem("inner_done"), n(i, 1, 1))
            dve.scalar_tensor_tensor(out=by_tile(inner_t), in0=by_tile(bank[2][:, :]),
                                     scalar=ret_c[:, 0:1], in1=tiled(const("tri_up")), op0=ALU.mult,
                                     op1=ALU.mult).then_inc(sem("inner_ready"), 1)
            split_lo(dve, hc(i, 3))
            normalise(0)
            drain_prob_t(0)
            dve.wait_ge(sem("kv_done"), n(i, 1, 1))
            earlier(dve, "ret_out_done", i, 1)
            dve.tensor_copy(ret_s[:, 0, :], bank[2][:, 0:DV_B]).then_inc(sem("ret_s_ready"), 1)
            for s in (1, 2):
                dve.wait_ge(sem("ret_s_ready"), n(i, 3, s))
                dve.scalar_tensor_tensor(out=ret_s[:, s, :], in0=ret_s[:, s - 1, :],
                                         scalar=ret_c[:, 4:5],
                                         in1=bank[2 + s // 2][:, (s % 2) * DV_B:(s % 2 + 1) * DV_B],
                                         op0=ALU.mult, op1=ALU.add).then_inc(sem("ret_s_ready"), 1)
            split_lo(dve, hc(i, 4))
            gated(0, 3)
            soft_max(1)
            split_lo(dve, hc(i, 5))
            normalise(1)
            drain_prob_t(1)
            split_lo(dve, hc(i, 6))
            dve.wait_ge(sem("ret_ssq"), n(i, 4, 4))
            dve.tensor_scalar(stat[:, 4:8], stat[:, 0:4], ret_c[:, 2:3], None, ALU.mult).then_inc(
                sem("ret_ms_ready"), 1)
            dve.wait_ge(sem("ret_rstd"), n(i, 1, 1))
            dve.tensor_scalar(stat[:, 8:12], stat[:, 4:8], ret_c[:, 3:4], None, ALU.mult).then_inc(
                sem("ret_scale_ready"), 1)
            split_lo(dve, hc(i, 7))
            gated(1, 6)
            for j in range(2):
                dve.wait_ge(sem("ret_turned"), n(i, 2, j + 1))
                dve.wait_ge(sem("l0_drained"), hc(i, 4 + j).count(1))
                dve.scalar_tensor_tensor(out=gate[:, 2 + j, :], in0=bank[4 + j][:, :],
                                         scalar=vec[:, ds(i * 2 + _V["ab_ret_norm"][0] + j, 1)],
                                         in1=gate[:, 2 + j, :], op0=ALU.mult, op1=ALU.mult).then_inc(
                    sem("y_made"), 1)

        def heads_pool(eng):
            def rotate(i):
                if not (isinstance(i, int) and i == 0):
                    earlier(eng, "rot_turned", i, 2)
                    earlier(eng, "k_dec_ready", i, 1)
                    passed(eng, "pool_passed")
                cos = const("cos").rearrange("p (t d) -> p t d", t=NT)
                sin = const("sin").rearrange("p (t d) -> p t d", t=NT)
                step = [0]

                def done(m):
                    step[0] += 1
                    m.then_inc(sem("rot_step"), 1)
                    eng.wait_ge(sem("rot_step"), n(i, 12, step[0]))
                    passed(eng, "pool_passed")

                for j in range(2):
                    x1 = qkvb[:, :, ds(i * P + j * 512, 64)]
                    x2 = qkvb[:, :, ds(i * P + j * 512 + 64, 64)]
                    lo, hi = rot[:, j, :, 0:64], rot[:, j, :, 64:P]
                    done(eng.tensor_tensor(lo, x1, cos, ALU.mult))
                    done(eng.tensor_tensor(rot_tmp, x2, sin, ALU.mult))
                    done(eng.tensor_tensor(lo, lo, rot_tmp, ALU.subtract))
                    done(eng.tensor_tensor(hi, x2, cos, ALU.mult))
                    done(eng.tensor_tensor(rot_tmp, x1, sin, ALU.mult))
                    done(eng.tensor_tensor(hi, hi, rot_tmp, ALU.add))
                    eng.sem_inc(sem("rot_ready"), 1)

            def store(i):
                for j in range(4):
                    eng.wait_ge(sem("y_made"), n(i, 4, j + 1))
                    row = i * (2 * P) + (j if j < 2 else 6 + j) * P
                    dst = y0_rows[row:row + P, :] if isinstance(i, int) else y0_rows[ds(row, P), :]
                    eng.dma_start(dst, gate[:, j, :]).then_inc(sem(f"y0_stored{j}"), 16)

            eng.wait_ge(sem("l0_drained"), N_HEADS)
            rotate(0)
            rotate(1)
            store(0)
            with eng.Fori(1, 3) as i:
                rotate(i + 1)
                store(i)
            store(3)

        def gates_sync(sp):
            load_chunk(sp, Chunk(N_BA), A["dn_w_in"][:, C_BA:C_BA + 64], cols=KT * 64)
            for j, col in enumerate((0, C_K1, C_V1, C_V1 + P)):
                load_chunk(sp, Chunk(N_FIRST + j), A["dn_w_in"][:, col:col + P])

        def gates_act(act):
            act.dma_start(k1, A["k1"]).then_inc(sem("head_cols_loaded"), 16)
            for j, name in enumerate(("dn_a_log", "dn_dt_bias")):
                act.dma_start(head_cols[0:H_V, j:j + 1], A[name]).then_inc(sem("head_cols_loaded"), 16)
            norm_stats_act(act, 1)
            norm_turn_act(act, 1, "dn_norm")
            c = Chunk(N_BA)
            split_hi(act, c.plus(2))
            act.wait_ge(sem("chunk_done"), c.count(1))
            act.wait_ge(sem("head_cols_loaded"), 48)
            act.activation(ba_t[0:H_V, :], bank[1][0:H_V, :], ACT.Sigmoid).then_inc(sem("softplus"), 1)
            act.activation(a_t[0:H_V, :], bank[1][H_V:2 * H_V, :], ACT.Identity,
                           bias=head_cols[0:H_V, 1:2]).then_inc(sem("softplus"), 1)
            act.activation(head_cols[0:H_V, 2:3], head_cols[0:H_V, 0:1], ACT.Exp).then_inc(
                sem("softplus"), 1)
            act.wait_ge(sem("softplus"), 2)
            act.activation(sp_1[0:H_V, :], a_t[0:H_V, :], ACT.Abs).then_inc(sem("softplus"), 1)
            act.wait_ge(sem("softplus"), 4)
            act.activation(sp_1[0:H_V, :], sp_1[0:H_V, :], ACT.Exp, scale=-1.0).then_inc(sem("softplus"), 1)
            act.wait_ge(sem("softplus"), 5)
            act.activation(sp_2[0:H_V, :], sp_1[0:H_V, :], ACT.Ln, bias=one_col[0:H_V, :]).then_inc(
                sem("softplus"), 1)
            split_hi(act, c.plus(3))
            conv_first_tap(act, 0, 0)
            act.wait_ge(sem("gates_turned"), 1)
            act.activation(gate_tab[:, 1].rearrange("p t h -> p (t h)"), bank[3][:, 0:P], ACT.Copy).then_inc(
                sem("g_n_ready"), 1)
            act.activation(g_n.rearrange("p t h -> p (t h)"), bank[3][:, P:2 * P], ACT.Copy).then_inc(
                sem("g_n_ready"), 1)
            conv_silu(act, 0, 0)
            split_hi(act, c.plus(4))
            conv_first_tap(act, 1, 0)
            act.wait_ge(sem("gates_turned"), 2)
            act.activation(gate_tab[:, 0].rearrange("p t h -> p (t h)"), bank[2][:, 0:P], ACT.Copy).then_inc(
                sem("tab_ready"), 1)
            act.activation(gate_tab[:, 4].rearrange("p t h -> p (t h)"), bank[2][:, P:2 * P], ACT.Exp).then_inc(
                sem("tab_ready"), 1)
            act.activation(sp_3[:, P:2 * P], bank[2][:, P:2 * P], ACT.Copy).then_inc(sem("tab_ready"), 1)
            act.wait_ge(sem("tab_ready"), 1)
            act.activation(sp_3[:, 0:P], gate_tab[:, 0].rearrange("p t h -> p (t h)"), ACT.Exp).then_inc(
                sem("tab_ready"), 1)
            act.wait_ge(sem("tab_steps"), 1)
            act.activation(gate_tab[:, 3].rearrange("p t h -> p (t h)"), sp_3[:, 2 * P:3 * P],
                           ACT.Exp).then_inc(sem("tab_ready"), 1)
            act.wait_ge(sem("gates_turned"), 3)
            act.activation(a_t[0:H_V, :], bank[3][0:H_V, :], ACT.Copy).then_inc(sem("tab_ready"), 1)
            act.wait_ge(sem("tab_ready"), 6)
            act.dma_start(g_rows, a_t[0:H_V, :]).then_inc(sem("g_rows_stored"), 16)
            conv_silu(act, 1, 0)
            split_hi(act, c.plus(5))
            conv_first_tap(act, 2, 0)
            conv_silu(act, 2, 0)
            split_hi(act, c.plus(6))
            conv_first_tap(act, 3, 0)
            conv_silu(act, 3, 0)

        def gates_dve(dve):
            norm_rows_dve(dve, 1)
            norm_turn_dve(dve, 1, "dn_norm")
            split_lo(dve, Chunk(N_BA + 2))
            dve.wait_ge(sem("softplus"), 6)
            dve.scalar_tensor_tensor(out=sp_2[0:H_V, :], in0=a_t[0:H_V, :], scalar=0.0, in1=sp_2[0:H_V, :],
                                     op0=ALU.max, op1=ALU.add).then_inc(sem("g_log"), 1)
            dve.wait_ge(sem("g_log"), 1)
            dve.tensor_scalar(sp_2[0:H_V, :], sp_2[0:H_V, :], head_cols[0:H_V, 2:3], -1.0, ALU.mult,
                              ALU.mult).then_inc(sem("g_log"), 1)
            split_lo(dve, Chunk(N_BA + 3))
            conv_taps(dve, 0, 0)
            split_lo(dve, Chunk(N_BA + 4))
            conv_taps(dve, 1, 0)
            dve.wait_ge(sem("tab_ready"), 3)
            dve.tensor_tensor(sp_3[:, 2 * P:3 * P], sp_3[:, P:2 * P],
                              gate_tab[:, 0].rearrange("p t h -> p (t h)"), ALU.subtract).then_inc(
                sem("tab_steps"), 1)
            dve.wait_ge(sem("tab_ready"), 4)
            dve.tensor_scalar(gate_tab[:, 2].rearrange("p t h -> p (t h)"), sp_3[:, 0:P], -1.0, None,
                              ALU.mult).then_inc(sem("tab_steps"), 1)
            split_lo(dve, Chunk(N_BA + 5))
            conv_taps(dve, 2, 0)
            split_lo(dve, Chunk(N_BA + 6))
            conv_taps(dve, 3, 0)
            dve.wait_ge(sem("tab_ready"), 5)
            dve.wait_ge(sem("tab_steps"), 2)

        def gates_pe(pe):
            norm_pe(pe, 1)
            t_products(pe, Chunk(N_BA), width=64)
            t_products(pe, Chunk(N_FIRST))
            pe.wait_ge(sem("g_log"), 2)
            for j, src in enumerate((ba_t, sp_2)):
                for t in range(NT):
                    m = pe.transpose(bank[3][:, j * P + t * H_V:j * P + (t + 1) * H_V],
                                     src[0:H_V, ts(t, P)], ident[0:H_V, 0:H_V])
            m.then_inc(sem("gates_turned"), 1)
            t_products(pe, Chunk(N_FIRST + 1))
            pe.wait_ge(sem("g_n_ready"), 2)
            g_cols = g_n.rearrange("p t h -> p (t h)")
            pe.matmul(bank[2][:, 0:P], const("tri_up"), g_cols, start=True, stop=True)
            pe.matmul(bank[2][:, P:2 * P], ones, g_cols, start=True, stop=True).then_inc(sem("gates_turned"), 1)
            pe.wait_ge(sem("tab_ready"), 1)
            for t in range(NT):
                m = pe.transpose(bank[3][0:H_V, ts(t, P)], gate_tab[:, 0, t, :], ident)
            m.then_inc(sem("gates_turned"), 1)
            t_products(pe, Chunk(N_FIRST + 2), free=(sem("conv_drained"), 1))
            t_products(pe, Chunk(N_FIRST + 3), free=(sem("conv_drained"), 2))
            pe.wait_ge(sem("tab_ready"), 6)

        def conv_chunk(j, g):
            if isinstance(g, int) and g == 0:
                return Chunk(N_FIRST + j)
            return Chunk(N_GROUPS - 6 + 2 + j, g, 6)

        def tap_col(tap, j, g):
            a = tap * 64 + (0, 16, 32, 33)[j]
            step = (1, 1, 2, 2)[j]
            if isinstance(g, int):
                return taps[:, a + step * g:a + step * g + 1]
            return taps[:, ds(g * step + a, 1)]

        def conv_first_tap(act, j, g):
            c = conv_chunk(j, g)
            act.wait_ge(sem("chunk_done"), c.count(1))
            act.activation(cs[:, j, :], bank[c.slot][:, :], ACT.Copy, scale=tap_col(3, j, g)).then_inc(
                sem("conv_started"), 1)

        def conv_taps(dve, j, g):
            c = conv_chunk(j, g)
            dve.wait_ge(sem("conv_started"), n(g, 4, j + 1))
            for back in (1, 2, 3):
                if back > 1:
                    dve.wait_ge(sem("conv_tap"), n(g, 8, 2 * j + back - 1))
                dve.scalar_tensor_tensor(out=cs[:, j, back:SEQ], in0=bank[c.slot][:, 0:SEQ - back],
                                         scalar=tap_col(3 - back, j, g), in1=cs[:, j, back:SEQ],
                                         op0=ALU.mult, op1=ALU.add).then_inc(
                    sem("conv_tap" if back < 3 else "conv_drained"), 1)

        def conv_silu(act, j, g):
            act.wait_ge(sem("conv_drained"), n(g, 4, j + 1))
            act.activation(cs[:, j, :], cs[:, j, :], ACT.Silu).then_inc(sem("conv_ready"), 1)
            if j < 2:
                act.wait_ge(sem("conv_ready"), n(g, 4, j + 1))
                act.activation(sq[:, j, :], cs[:, j, :], ACT.Square).then_inc(sem("sq_ready"), 1)

        WORK = ((2, 3), (4, 5))
        OUTB = (6, 7)
        GAPS = 31

        def gap_at(j):
            return 16 + (80 * j) // GAPS

        def group_chunk(g, k):
            return Chunk(N_GROUPS + k, g, 6)

        def group_sync(sp, g, last=False):
            cols = [C_Z1, C_Z1 + P, P, C_K1 + P, C_V1 + 256, C_V1 + 384]
            per = [256, 256, 128, 128, 256, 256]
            for k in range(2 if last else 6):
                a = g * per[k] + cols[k]
                src = A["dn_w_in"][:, a:a + P] if isinstance(g, int) else A["dn_w_in"][:, ds(a, P)]
                load_chunk(sp, group_chunk(g, k), src)

        def group_pe(pe, g, last=False):
            end = 32 if last else 96
            at_k = [0]

            def products(upto):
                while at_k[0] < min(upto, end):
                    k, a = divmod(at_k[0], KT)
                    b = min(KT, a + min(upto, end) - at_k[0])
                    free = {0: (sem("conv_drained"), n(g, 4, 3)), 1: (sem("conv_drained"), n(g, 4, 4)),
                            2: (sem("z_ready"), n(g, 2, 1)), 3: (sem("z_ready"), n(g, 2, 2)),
                            4: (sem("conv_drained"), n(g, 4, 5)), 5: (sem("conv_drained"), n(g, 4, 6))}[k]
                    t_products(pe, group_chunk(g, k), a, b, free=free)
                    at_k[0] += b - a

            step = [0]

            def gap():
                step[0] += 1
                products(gap_at(step[0]))

            pe.wait_ge(sem("sq_ready"), n(g, 2, 2))
            earlier(pe, "y1_made", g, 2)
            pe.matmul(bank[4][:, :], ones, sq[:, 1, :], start=True, stop=True).then_inc(sem("ssq_done"), 1)
            pe.matmul(bank[2][:, :], ones, sq[:, 0, :], start=True, stop=True).then_inc(sem("ssq_done"), 1)
            pe.wait_ge(sem("conv_ready"), n(g, 4, 3))
            for t in range(NT):
                m = pe.transpose(bank[5][:, ts(t, P)], cs[:, 2, ts(t, P)], ident)
            m.then_inc(sem("v_turned0"), 1)
            products(8)
            pe.wait_ge(sem("kn_ready"), n(g, 1, 1))
            earlier(pe, "on_ready", g, 2)
            for t in range(NT):
                m = pe.matmul(bank[6][:, ts(t, P)], kn[:, ts(t, P)], kn[:, ts(t, P)], start=True, stop=True)
            m.then_inc(sem("kk_done"), 1)
            for t in range(NT):
                m = pe.transpose(bank[3][:, ts(t, P)], kn[:, ts(t, P)], ident)
            m.then_inc(sem("k_turned"), 1)
            pe.wait_ge(sem("qn_ready"), n(g, 1, 1))
            for t in range(NT):
                m = pe.matmul(bank[7][:, ts(t, P)], kn[:, ts(t, P)], qn[:, ts(t, P)], start=True, stop=True)
            m.then_inc(sem("kq_done"), 1)
            pe.wait_ge(sem("conv_ready"), n(g, 4, 4))
            for t in range(NT):
                m = pe.transpose(bank[2][:, ts(t, P)], cs[:, 3, ts(t, P)], ident)
            m.then_inc(sem("v_turned1"), 1)
            products(16)
            for e in range(2):
                pe.wait_ge(sem("inv_p_ready"), n(g, 14, 2 * (1) - 1 + e))
                if e == 0:
                    pe.wait_ge(sem("k_rows_ready"), n(g, 1, 1))
                else:
                    pe.wait_ge(sem("v_n_ready0"), n(g, 1, 1))
                for t in range(NT):
                    m = pe.transpose(bank[WORK[e][1]][:, ts(t, P)], inv_p[:, e, ts(t, P)], ident)
                m.then_inc(sem("inv_turned"), 1)
            gap()
            pe.wait_ge(sem("v_n_ready1"), n(g, 1, 1))
            for L in range(len(LEVELS)):
                for e in range(2):
                    pe.wait_ge(sem("inv_t_ready"), n(g, 12, 2 * (L + 1) - 1 + e))
                    for t in range(NT):
                        m = pe.matmul(bank[WORK[e][0]][:, ts(t, P)], f_up[:, e, ts(t, P)],
                                      inv_t[:, e, ts(t, P)], start=True, stop=True)
                    m.then_inc(sem("z_done"), 1)
                gap()
                for e in range(2):
                    pe.wait_ge(sem("z_m_ready"), n(g, 12, 2 * (L + 1) - 1 + e))
                    for t in range(NT):
                        m = pe.matmul(bank[WORK[e][1]][:, ts(t, P)], z_m[:, e, ts(t, P)],
                                      inv_p[:, e, ts(t, P)], start=True, stop=True)
                    m.then_inc(sem("zp_done"), 1)
                gap()
                if L < len(LEVELS) - 1:
                    for e in range(2):
                        pe.wait_ge(sem("inv_p_ready"), n(g, 14, 2 * (L + 2) - 1 + e))
                        for t in range(NT):
                            m = pe.transpose(bank[WORK[e][0]][:, ts(t, P)], inv_p[:, e, ts(t, P)], ident)
                        m.then_inc(sem("inv_turned"), 1)
                    gap()
            for t in range(NT):
                if t:
                    for e in range(2):
                        pe.wait_ge(sem("state_ready"), n(g, 6, 2 * (t) - 1 + e))
                        pe.matmul(bank[WORK[e][0]][:, 0:P], kn[:, ts(t, P)], state[:, e, :], start=True,
                                  stop=True).then_inc(sem("ks_done"), 1)
                        pe.matmul(bank[OUTB[e]][:, ts(t, P)], q_dec[:, e, ts(t, P)], state[:, e, :],
                                  start=True, stop=False)
                    gap()
                for e in range(2):
                    if t:
                        pe.wait_ge(sem("r_ready"), n(g, 6, 2 * (t) - 1 + e))
                    else:
                        pe.wait_ge(sem("inv_p_ready"), n(g, 14, 2 * (7) - 1 + e))
                        pe.wait_ge(sem("attn_ready"), n(g, 2, e + 1))
                    pe.matmul(bank[WORK[e][1]][:, 0:P], inv_p[:, e, ts(t, P)],
                              r_n[:, e, :] if t else v_n[:, e, 0, :], start=True, stop=True).then_inc(
                        sem("tr_done"), 1)
                gap()
                for e in range(2):
                    pe.wait_ge(sem("v_new_ready"), n(g, 8, 2 * (t + 1) - 1 + e))
                    if t < NT - 1:
                        if t == 0:
                            pe.wait_ge(sem("k_tail_ready"), n(g, 2, e + 1))
                            pe.wait_ge(sem("q_dec_ready"), n(g, 2, e + 1))
                            pe.wait_ge(sem("attn_ready"), n(g, 2, 2))
                        pe.matmul(bank[WORK[e][0]][:, 0:P], k_tail[:, e, t, :], v_new[:, e, :], start=True,
                                  stop=True).then_inc(sem("kv1_done"), 1)
                    m = pe.matmul(bank[OUTB[e]][:, ts(t, P)], attn_t[:, e, ts(t, P)], v_new[:, e, :],
                                  start=(t == 0), stop=True)
                    m.then_inc(sem("o_done"), 1)
                gap()
            for e in range(2):
                pe.wait_ge(sem("on_ready"), n(g, 2, e + 1))
                for t in range(NT):
                    m = pe.transpose(bank[WORK[e][1]][:, ts(t, P)], o_n[:, e, ts(t, P)], ident)
                m.then_inc(sem("o_turned"), 1)
                if e == 0:
                    gap()
            products(96)

        def crossings(g, last):
            end = 32 if last else 96
            return [[k for k in range(6) if (k + 1) * KT <= min(gap_at(j), end)
                     and not (k + 1) * KT <= min(gap_at(j - 1) if j > 1 else 16, end)]
                    for j in range(1, GAPS + 1)]

        def group_act(act, g, last=False):
            pending = []

            def finish(k):
                c = group_chunk(g, k)
                split_hi(act, c.plus(2))
                if k < 2:
                    act.wait_ge(sem("chunk_done"), c.count(1))
                    earlier(act, "y1_made", g, 2)
                    act.activation(zs[:, k, :], bank[c.slot][:, :], ACT.Silu).then_inc(sem("z_ready"), 1)
                else:
                    if k < 4:
                        act.wait_ge(sem("kq_done"), n(g, 1, 1))
                    conv_first_tap(act, k - 2, g + 1)
                    pending.append(k - 2)

            def silus():
                while pending:
                    conv_silu(act, pending.pop(0), g + 1)

            cross = crossings(g, last)
            step = [0]

            def gap():
                silus()
                step[0] += 1
                for k in cross[step[0] - 1]:
                    finish(k)

            earlier(act, "qn_ready", g, 1)
            for j, b in ((1, 4), (0, 2)):
                act.wait_ge(sem("ssq_done"), n(g, 2, 2 - j))
                rstd(act, rs[:, j, :], bank[b][:, :], 1.0, "group_ln_done",
                     n(g, 4, 2 - j)).then_inc(sem("l2_ready"), 1)
            act.wait_ge(sem("v_turned0"), n(g, 1, 1))
            act.activation(v_n[:, 0], by_tile(bank[5][:, :]), ACT.Copy).then_inc(sem("v_n_ready0"), 1)
            for e in range(2):
                act.wait_ge(sem("dec_log"), n(g, 2, e + 1))
                act.activation(dec[:, e, :], dec[:, e, :], ACT.Exp).then_inc(sem("dec_ready"), 1)
            earlier(act, "q_dec_ready", g, 2)
            for e in range(2):
                act.activation(eg[:, e, :], g_row[:, e, :], ACT.Exp).then_inc(sem("eg_ready"), 1)
            act.wait_ge(sem("k_turned"), n(g, 1, 1))
            act.activation(k_rows, by_tile(bank[3][:, :]), ACT.Copy).then_inc(sem("k_rows_ready"), 1)
            act.wait_ge(sem("v_turned1"), n(g, 1, 1))
            act.activation(v_n[:, 1], by_tile(bank[2][:, :]), ACT.Copy).then_inc(sem("v_n_ready1"), 1)

            def drain_inv(e, level):
                b = WORK[e][1] if level == 0 else WORK[e][0]
                act.wait_ge(sem("inv_turned"), n(g, 12, 2 * (level + 1) - 1 + e))
                act.activation(inv_t[:, e, :], bank[b][:, :], ACT.Copy).then_inc(sem("inv_t_ready"), 1)

            finish(0)
            for e in range(2):
                drain_inv(e, 0)
            gap()
            for L in range(len(LEVELS)):
                gap()
                gap()
                if L < len(LEVELS) - 1:
                    for e in range(2):
                        drain_inv(e, L + 1)
                    gap()
            for t in range(NT):
                if t:
                    gap()
                for e in range(2):
                    act.wait_ge(sem("tr_done"), n(g, 8, 2 * (t + 1) - 1 + e))
                    if t:
                        act.wait_ge(sem("o_done"), n(g, 8, 2 * (t) - 1 + e))
                    act.activation(v_new[:, e, :], bank[WORK[e][1]][:, 0:P], ACT.Copy,
                                   scale=gt[:, 1, t, e:e + 1]).then_inc(sem("v_new_ready"), 1)
                gap()
                gap()
            for e in range(2):
                act.wait_ge(sem("o_done"), n(g, 8, 2 * (NT) - 1 + e))
                for t in range(NT):
                    act.activation(o_n[:, e, ts(t, P)], bank[OUTB[e]][:, ts(t, P)], ACT.Square,
                                   accum_out=o_stat[:, e, 0, t:t + 1]).then_inc(sem("o_ssq"), 1)
                act.wait_ge(sem("o_ssq"), n(g, 8, 4 * e + 4))
                rstd(act, o_stat[:, e, 1, :], o_stat[:, e, 0, :], 1.0 / P, "group_ln_done",
                     n(g, 4, e + 3)).then_inc(
                    sem("o_rstd"), 1)
                if e == 0:
                    gap()
            while step[0] < GAPS:
                gap()
            silus()

        def group_dve(dve, g, last=False):
            def finish(k):
                split_lo(dve, group_chunk(g, k + 2))
                if k >= 2:
                    conv_taps(dve, k - 2, g + 1)

            cross = crossings(g, last)
            step = [0]

            def gap():
                step[0] += 1
                for k in cross[step[0] - 1]:
                    finish(k)

            cols = gate_tab[:, :, :, 2 * g:2 * g + 2] if isinstance(g, int) else \
                gate_tab[:, :, :, ds(g * 2, 2)]
            flat = "p k t h -> p (k t) h"
            earlier(dve, "k_tail_ready", g, 2)
            dve.tensor_copy(gt.rearrange(flat), cols.rearrange(flat)).then_inc(sem("gt_ready"), 1)
            dve.wait_ge(sem("gt_ready"), n(g, 1, 1))
            dve.wait_ge(sem("g_row_loaded"), n(g, 16, 16))
            for e in range(2):
                for t in range(NT):
                    m = dve.scalar_tensor_tensor(out=dec[:, e, ts(t, P)], in0=g_row[:, e, ts(t, P)],
                                                 scalar=gt[:, 0, t, e:e + 1], in1=k1c("hide_up"),
                                                 op0=ALU.subtract, op1=ALU.add)
                m.then_inc(sem("dec_log"), 1)
            dve.wait_ge(sem("l2_ready"), n(g, 2, 1))
            dve.tensor_tensor(kn, cs[:, 1, :], rs[:, 1, :], ALU.mult).then_inc(sem("kn_ready"), 1)
            dve.wait_ge(sem("l2_ready"), n(g, 2, 2))
            dve.scalar_tensor_tensor(out=qn, in0=cs[:, 0, :], scalar=P ** -0.5, in1=rs[:, 0, :],
                                     op0=ALU.mult, op1=ALU.mult).then_inc(sem("qn_ready"), 1)
            for e in range(2):
                dve.wait_ge(sem("kk_done"), n(g, 1, 1))
                dve.wait_ge(sem("dec_ready"), n(g, 2, e + 1))
                for t in range(NT):
                    m = dve.scalar_tensor_tensor(out=f_up[:, e, ts(t, P)], in0=bank[6][:, ts(t, P)],
                                                 scalar=gt[:, 1, t, e:e + 1], in1=dec[:, e, ts(t, P)],
                                                 op0=ALU.mult, op1=ALU.mult)
                m.then_inc(sem("f_ready"), 1)
                dve.wait_ge(sem("f_ready"), n(g, 2, e + 1))
                dve.tensor_tensor(by_tile(inv_p[:, e, :]), by_tile(f_up[:, e, :]), tiled(k1c("pair_up")),
                                  ALU.mult).then_inc(sem("pair_ready"), 1)
                dve.wait_ge(sem("pair_ready"), n(g, 2, e + 1))
                dve.tensor_tensor(by_tile(inv_p[:, e, :]), tiled(ident), by_tile(inv_p[:, e, :]),
                                  ALU.subtract).then_inc(sem("inv_p_ready"), 1)
            for e in range(2):
                dve.wait_ge(sem("kq_done"), n(g, 1, 1))
                dve.tensor_tensor(attn_t[:, e, :], bank[7][:, :], dec[:, e, :], ALU.mult).then_inc(
                    sem("attn_ready"), 1)
            finish(0)
            gap()
            for L in range(len(LEVELS)):
                for e in range(2):
                    dve.wait_ge(sem("z_done"), n(g, 12, 2 * (L + 1) - 1 + e))
                    dve.tensor_tensor(by_tile(z_m[:, e, :]), by_tile(bank[WORK[e][0]][:, :]),
                                      tiled(k1c("levels")[:, ts(L, P)]), ALU.mult).then_inc(
                        sem("z_m_ready"), 1)
                gap()
                for e in range(2):
                    dve.wait_ge(sem("zp_done"), n(g, 12, 2 * (L + 1) - 1 + e))
                    dve.tensor_tensor(inv_p[:, e, :], inv_p[:, e, :], bank[WORK[e][1]][:, :],
                                      ALU.subtract).then_inc(sem("inv_p_ready"), 1)
                gap()
                if L < len(LEVELS) - 1:
                    gap()
            for t in range(NT):
                if t:
                    for e in range(2):
                        dve.wait_ge(sem("ks_done"), n(g, 6, 2 * (t) - 1 + e))
                        dve.scalar_tensor_tensor(out=r_n[:, e, :], in0=bank[WORK[e][0]][:, 0:P],
                                                 scalar=gt[:, 2, t, e:e + 1], in1=v_n[:, e, t, :],
                                                 op0=ALU.mult, op1=ALU.add).then_inc(sem("r_ready"), 1)
                    gap()
                gap()
                if t < NT - 1:
                    for e in range(2):
                        dve.wait_ge(sem("kv1_done"), n(g, 6, 2 * (t + 1) - 1 + e))
                        if t == 0:
                            m = dve.tensor_copy(state[:, e, :], bank[WORK[e][0]][:, 0:P])
                        else:
                            m = dve.scalar_tensor_tensor(out=state[:, e, :], in0=state[:, e, :],
                                                         scalar=gt[:, 4, t, e:e + 1],
                                                         in1=bank[WORK[e][0]][:, 0:P], op0=ALU.mult,
                                                         op1=ALU.add)
                        m.then_inc(sem("state_ready"), 1)
                gap()
            for e in range(2):
                dve.wait_ge(sem("o_rstd"), n(g, 2, e + 1))
                dve.tensor_tensor(by_tile(o_n[:, e, :]), by_tile(bank[OUTB[e]][:, :]),
                                  spread(o_stat[:, e, 1, :]), ALU.mult).then_inc(sem("on_ready"), 1)
                if e == 0:
                    gap()
            while step[0] < GAPS:
                gap()
            dve.wait_ge(sem("z_ready"), n(g, 2, 2))
            for e in range(2):
                dve.wait_ge(sem("o_turned"), n(g, 2, e + 1))
                earlier(dve, f"y1_stored{e}", g, 16)
                dve.scalar_tensor_tensor(out=y_out[:, e, :], in0=bank[WORK[e][1]][:, :],
                                         scalar=vcol("dn_out_norm"), in1=zs[:, e, :], op0=ALU.mult,
                                         op1=ALU.mult).then_inc(sem("y1_made"), 1)

        def g_row_load(eng, g):
            src = g_rows[2 * g:2 * g + 2, :] if isinstance(g, int) else g_rows[ds(g * 2, 2), :]
            eng.dma_start(g_row, src.rearrange("(o h) s -> o h s", o=1).broadcast_to([P, 2, SEQ])).then_inc(
                sem("g_row_loaded"), 16)

        def group_pool(eng, g, last=False):
            for e in range(2):
                eng.wait_ge(sem("eg_ready"), n(g, 2, e + 1))
                eng.wait_ge(sem("qn_ready"), n(g, 1, 1))
                eng.tensor_tensor(q_dec[:, e, :], qn, eg[:, e, :], ALU.mult).then_inc(sem("q_dec_ready"), 1)
            eng.wait_ge(sem("k_rows_ready"), n(g, 1, 1))
            eng.wait_ge(sem("gt_ready"), n(g, 1, 1))
            for e in range(2):
                eng.tensor_tensor(k_tail[:, e], k_rows, spread(gt[:, 3, :, e]), ALU.mult).then_inc(
                    sem("k_tail_ready"), 1)
            if not last:
                g_row_load(eng, g + 1)
            for e in range(2):
                eng.wait_ge(sem("y1_made"), n(g, 2, e + 1))
                row = g * (2 * P) + e * P
                dst = y1_rows[row:row + P, :] if isinstance(g, int) else y1_rows[ds(row, P), :]
                eng.dma_start(dst, y_out[:, e, :]).then_inc(sem(f"y1_stored{e}"), 16)

        block = ctx.enter_context(nc.Block())

        @block.sync
        def _(sp):
            pre_sync(sp)
            heads_sync(sp)
            out_sync(sp, "out0")
            gates_sync(sp)
            group_sync(sp, 0)
            with sp.Fori(1, H_QK - 1) as g:
                group_sync(sp, g)
            group_sync(sp, H_QK - 1, last=True)
            out_sync(sp, "out1a")
            out_sync(sp, "out1b")
            sp.wait_ge(sem("out_stored"), 64)

        @block.gpsimd
        def _(eng):
            heads_pool(eng)
            for j in range(4):
                eng.wait_ge(sem(f"y0_stored{j}"), 64)
            out_pool(eng, "out0")
            eng.wait_ge(sem("h_mid_stored"), 64)
            eng.wait_ge(sem("g_rows_stored"), 16)
            g_row_load(eng, 0)
            group_pool(eng, 0)
            with eng.Fori(1, H_QK - 1) as g:
                group_pool(eng, g)
            group_pool(eng, H_QK - 1, last=True)
            for e in range(2):
                eng.wait_ge(sem(f"y1_stored{e}"), 16 * H_QK)
            out_pool(eng, "out1a")
            out_pool(eng, "out1b")

        @block.scalar
        def _(act):
            pre_act(act)
            heads_act(act)
            out_act(act, "out0")
            act.wait_ge(sem("block_summed"), 16)
            gates_act(act)
            group_act(act, 0)
            with act.Fori(1, H_QK - 1) as g:
                group_act(act, g)
            group_act(act, H_QK - 1, last=True)
            out_act(act, "out1a")
            out_act(act, "out1b")

        @block.vector
        def _(dve):
            pre_dve(dve)
            heads_dve(dve)
            out_dve(dve, "out0")
            gates_dve(dve)
            group_dve(dve, 0)
            with dve.Fori(1, H_QK - 1) as g:
                group_dve(dve, g)
            group_dve(dve, H_QK - 1, last=True)
            out_dve(dve, "out1a")
            out_dve(dve, "out1b")

        @block.tensor
        def _(pe):
            pre_pe(pe)
            heads_pe(pe)
            pe.wait_ge(sem("l0_drained"), N_OUT0)
            out_pe(pe, "out0")
            gates_pe(pe)
            group_pe(pe, 0)
            with pe.Fori(1, H_QK - 1) as g:
                group_pe(pe, g)
            group_pe(pe, H_QK - 1, last=True)
            pe.wait_ge(sem("z_ready"), 2 * H_QK)
            pe.wait_ge(sem("y1_made"), 2 * H_QK)
            out_pe(pe, "out1a")
            pe.wait_ge(sem("block_summed"), 32)
            out_pe(pe, "out1b")


_SHAPES = {"x": (SEQ, DM), "ab_norm": (16, P), "ab_w_in": None, "ab_kv_norm": (2, P), "ab_w_uk": None,
           "ab_w_uv": (H_A * D_C, P), "ab_q_norm": (1, P), "ab_k_norm": (1, P), "ab_ret_norm": (8, P),
           "ab_w_out": None, "dn_norm": (16, P), "dn_w_in": None, "dn_conv": (256, P),
           "dn_a_log": (H_V, 1), "dn_dt_bias": (H_V, 1), "dn_out_norm": (1, P), "dn_w_out": None}


def kernel(**inputs):
    import concourse.bacc as bacc
    from concourse.bass_utils import run_bass_kernel_spmd

    nc = bacc.Bacc("TRN2", target_bir_lowering=False, num_devices=1)
    arrays, aps = {}, {}
    for name, shape in _SHAPES.items():
        a = np.asarray(inputs[name])
        arrays[name] = np.ascontiguousarray(a.reshape(shape or a.shape[1:]))
    arrays["k0"], arrays["k1"] = constant_tables()
    for name, a in arrays.items():
        aps[name] = nc.dram_tensor(name, a.shape, F32, kind="ExternalInput").ap()
    aps["out"] = nc.dram_tensor("out", (SEQ, DM), F32, kind="ExternalOutput").ap()
    build(nc, aps)
    r = run_bass_kernel_spmd(nc, [arrays], core_ids=[0])
    return r.results[0]["out"].reshape(1, SEQ, DM)
```

```python
import math
from contextlib import ExitStack

import numpy as np

import concourse.bass as bass
from concourse import mybir

F32, F32R = mybir.dt.float32, mybir.dt.float32r
ALU, ACT = mybir.AluOpType, mybir.ActivationFunctionType
ds, ts = bass.ds, bass.ts

P = 128
SEQ, DM = 512, 2048
NT = SEQ // P
KT = DM // P
H_A, D_C, H_I, D_I, TOPK = 8, 256, 8, 64, 128
H_B, DK_B, DV_B = 4, 128, 256
H_QK, H_V = 16, 32
EPS = 1e-6
CH = 2048

C_QA = 0
C_C = C_QA + H_A * P
C_QI = C_C + D_C
C_KI = C_QI + H_I * D_I
C_W = C_KI + D_I
C_QKVB = C_W + H_I
C_GATE = C_QKVB + 2 * H_B * DK_B + H_B * DV_B
C_K1 = H_QK * P
C_V1 = 2 * H_QK * P
C_Z1 = C_V1 + H_V * P
C_BA = C_Z1 + H_V * P

N_KI, N_QI, N_QKVB = 2, 3, 7
N_HEADS = N_QKVB + 16
N_OUT0 = N_HEADS + 24
N_BA = N_OUT0 + 16
N_FIRST = N_BA + 1
N_GROUPS = N_FIRST + 4
N_OUT1A = N_GROUPS + 6 * (H_QK - 1) + 2
N_OUT1B = N_OUT1A + 16
N_END = N_OUT1B + 16

HIDE = -1.0e30
TAKEN = -3.0e38
LEVELS = (2, 4, 8, 16, 32, 64)

_K = {}
_n = 0
for _name, _w in (("ident", P), ("ones", P), ("hide_low", P), ("tri_up", P), ("cos", NT * 64),
                  ("sin", NT * 64), ("ret_in", H_B), ("ret_kd", H_B), ("ret_ms", H_B),
                  ("ret_out", H_B), ("ret_cd", H_B)):
    _K[_name] = (_n, _w)
    _n += _w
K0_COLS = _n
_K1 = {}
_n = 0
for _name, _w in (("hide_up", P), ("pair_up", P), ("levels", P * len(LEVELS))):
    _K1[_name] = (_n, _w)
    _n += _w
K1_COLS = _n


def constant_tables():
    i = np.arange(P)
    k0 = np.zeros((P, K0_COLS), np.float32)
    k1 = np.zeros((P, K1_COLS), np.float32)

    def put(name, value):
        table, where = (k0, _K) if name in _K else (k1, _K1)
        a, w = where[name]
        table[:, a:a + w] = value

    put("ident", np.eye(P))
    put("ones", 1.0)
    put("hide_low", np.where(i[None, :] <= i[:, None], 0.0, HIDE))
    put("tri_up", i[None, :] >= i[:, None])
    pos = np.arange(SEQ, dtype=np.float32)
    inv = (1.0 / (np.float32(10000.0) ** np.linspace(0, 1, 64, dtype=np.float32))).astype(np.float32)
    ang = (pos[:, None] * inv[None, :]).astype(np.float32)
    for name, f in (("cos", np.cos), ("sin", np.sin)):
        put(name, f(ang).reshape(NT, P, 64).transpose(1, 0, 2).reshape(P, NT * 64))
    lg = np.log1p(-np.exp2(-5.0 - np.arange(H_B)))[None, :]
    col = i[:, None].astype(np.float64)
    put("ret_in", DK_B ** -0.5 * np.exp(-(col + 1) * lg))
    put("ret_kd", DK_B ** -0.5 * np.exp((P - 1 - col) * lg))
    put("ret_ms", np.exp(2 * (col + 1) * lg) / DV_B)
    put("ret_out", np.exp((col + 1) * lg))
    put("ret_cd", np.exp(P * lg) + 0 * col)
    put("hide_up", np.where(i[None, :] >= i[:, None], 0.0, HIDE))
    put("pair_up", (i[None, :] // 2 == i[:, None] // 2) & (i[None, :] > i[:, None]))
    a, _ = _K1["levels"]
    for n, b in enumerate(LEVELS):
        row, c = i[:, None] // b, i[None, :] // b
        k1[:, a + n * P:a + (n + 1) * P] = (row % 2 == 1) & (c == row - 1)
    return k0, k1


_V = {"ab_norm": (0, 16), "dn_norm": (16, 16), "ab_kv_norm": (32, 2), "ab_q_norm": (34, 1),
      "ab_k_norm": (35, 1), "ab_ret_norm": (36, 8), "dn_out_norm": (44, 1)}
V_ROWS = 45


def build(nc, A):
    ctx = ExitStack()
    with ctx:
        def sb(name, shape, dt=F32):
            return ctx.enter_context(nc.sbuf_tensor(name, shape, dt))

        sems = {}

        def sem(name):
            if name not in sems:
                sems[name] = ctx.enter_context(nc.semaphore(name))
            return sems[name]

        def scratch(name, shape):
            return nc.dram_tensor(name, shape, F32).ap()

        x_hi = sb("x_hi", [P, KT, SEQ], F32R)
        x_lo = sb("x_lo", [P, KT, SEQ], F32R)
        w_raw = sb("w_raw", [P, 2, CH])
        w_hi = sb("w_hi", [P, 2, CH], F32R)
        w_lo = sb("w_lo", [P, 2, CH], F32R)
        pool_cols = 24400
        pool = sb("pool", [P, pool_cols])
        bank = [ctx.enter_context(nc.psum_tensor(f"bank{i}", [P, 512], F32)) for i in range(8)]

        def region(start):
            at = [start]

            def take(*shape):
                n = int(np.prod(shape))
                a = pool[:, at[0]:at[0] + n]
                at[0] += n
                assert at[0] <= pool_cols, at[0]
                if len(shape) == 2:
                    a = a.rearrange("p (a b) -> p a b", a=shape[0])
                elif len(shape) == 3:
                    a = a.rearrange("p (a b c) -> p a b c", a=shape[0], b=shape[1])
                return a
            return take, at

        take, at = region(0)
        k0 = take(K0_COLS)
        vec = take(V_ROWS)
        kq_gain = take(1)
        eps_col, ln_col, one_col = take(1), take(1), take(1)
        taps = take(256)
        ssq_parts = take(16)
        stat = take(16)
        rows_in = take(P)
        shared_end = at[0]

        def const(name):
            a, w = _K[name]
            return k0[:, a:a + w]

        ident, ones = const("ident"), const("ones")

        def vcol(name, j=0):
            a = _V[name][0] + j
            return vec[:, a:a + 1]

        take, _ = region(shared_end)
        rows = take(NT, DM)
        square_out = take(DM)
        diag = take(NT, P)
        take, _ = region(shared_end + NT * DM)
        y_stage = take(KT, SEQ)
        resid = take(2, NT, 512)

        take, at = region(shared_end)
        qkvb = take(NT, 2048)
        l0_start = at[0]
        bias = take(1280)
        c_n = take(NT, D_C)
        key_t = take(SEQ)
        after_keep = at[0]
        ki_t = take(SEQ)
        wi_t = take(SEQ)
        wi_n = take(NT, H_I)
        qi_t = take(2, SEQ)
        relu_s = take(2, 1152)
        top8 = take(3, 8)
        c_t = take(2, SEQ)
        k_n = take(NT, P)
        w_uk = take(2, P)
        take, at = region(after_keep)
        q_t = take(SEQ)
        q_sq = take(SEQ)
        prob = take(1280)
        prob_t = take(1280)
        lat_t = take(2, SEQ)
        w_uv = take(2, 2, P)
        rot = take(2, NT, P)
        rot_tmp = take(NT, 64)
        rot_t = take(2, SEQ)
        k_dec = take(NT, P)
        ret_s = take(3, DV_B)
        ret_n = take(NT, DV_B)
        gate = take(4, SEQ)
        soft = take(24)
        ret_c = take(5)
        inner_t = rot_t[:, 1, :]

        off = [0, 128, 384, 768]
        wid = [128, 256, 384, 512]
        toff = [0, 512, 896, 1152]

        take, at = region(shared_end)
        cs = take(4, SEQ)
        zs = take(2, SEQ)
        sq = take(2, SEQ)
        rs = take(2, SEQ)
        qn, kn = take(SEQ), take(SEQ)
        k_rows = take(NT, P)
        g_row = take(2, SEQ)
        dec = take(2, SEQ)
        eg = take(2, SEQ)
        q_dec = take(2, SEQ)
        k_tail = take(2, NT, P)
        attn_t = take(2, SEQ)
        f_up = take(2, SEQ)
        inv_p = take(2, SEQ)
        inv_t = take(2, SEQ)
        z_m = take(2, SEQ)
        v_n = take(2, NT, P)
        r_n = take(2, P)
        v_new = take(2, P)
        state = take(2, P)
        o_n = take(2, SEQ)
        y_out = take(2, SEQ)
        o_stat = take(2, 2, NT)
        k1 = take(K1_COLS)
        gate_tab = take(5, NT, H_V)
        gt = take(5, NT, 2)
        take, at = region(shared_end + NT * DM)
        ba_t = take(SEQ)
        a_t = take(SEQ)
        sp_1, sp_2, sp_3 = take(SEQ), take(SEQ), take(SEQ)
        head_cols = take(4)
        g_n = take(NT, H_V)

        def k1c(name):
            a, w = _K1[name]
            return k1[:, a:a + w]

        def tiled(ap, n=NT):
            return ap.rearrange("p (o c) -> p o c", o=1).broadcast_to([P, n, P])

        def by_tile(ap):
            return ap.rearrange("p (t c) -> p t c", t=NT)

        def spread(cols, w=P):
            n = cols.shape[1]
            return cols.rearrange("p (t o) -> p t o", o=1).broadcast_to([P, n, w])

        y0_rows = scratch("y0", (KT * P, SEQ))
        y1_rows = scratch("y1", (H_V * P, SEQ))
        y0 = y0_rows.rearrange("(k p) s -> k p s", p=P)
        y1 = y1_rows.rearrange("(k p) s -> k p s", p=P)
        _a = _K["ret_in"][0]
        ret_tab = k0[:, _a:_a + 5 * H_B].rearrange("p (k h) -> p k h", h=H_B)
        h_mid = scratch("h_mid", (SEQ, DM))
        g_rows = scratch("g_rows", (H_V, SEQ))

        class Chunk:

            def __init__(self, base, i=0, per=0):
                assert per % 2 == 0 or isinstance(i, int)
                if isinstance(i, int):
                    base, i, per = base + per * i, 0, 0
                self.base, self.i, self.per = base, i, per
                self.slot = base % 2

            def count(self, d=0):
                return self.base + d if self.per == 0 else self.i * self.per + (self.base + d)

            def loads(self):
                h = self.base // 2 + 1
                return 16 * h if self.per == 0 else self.i * (8 * self.per) + 16 * h

            def plus(self, d):
                return Chunk(self.base + d, self.i, self.per)

        def load_chunk(sp, c, src, cols=CH, kts=KT):
            if c.base >= 2:
                sp.wait_ge(sem("lo_ready"), c.count(-1))
            w = cols // kts
            dst = w_raw[:, c.slot, 0:cols].rearrange("p (k n) -> p k n", n=w)
            sp.dma_start(dst, src.rearrange("(k p) n -> p k n", p=P)).then_inc(
                sem(f"raw_loaded{c.slot}"), 16)

        def split_hi(act, c, cols=CH):
            act.wait_ge(sem(f"raw_loaded{c.slot}"), c.loads())
            if c.base >= 2:
                act.wait_ge(sem("chunk_done"), c.count(-1))
            act.activation(w_hi[:, c.slot, 0:cols], w_raw[:, c.slot, 0:cols], ACT.Copy).then_inc(
                sem("hi_ready"), 1)

        def split_hi_half(act, c, half):
            if half == 0:
                act.wait_ge(sem(f"raw_loaded{c.slot}"), c.loads())
                act.wait_ge(sem("chunk_done"), c.count(-1))
            part = slice(half * CH // 2, (half + 1) * CH // 2)
            m = act.activation(w_hi[:, c.slot, part], w_raw[:, c.slot, part], ACT.Copy)
            if half:
                m.then_inc(sem("hi_ready"), 1)

        def split_lo_half(dve, c, half):
            if half == 0:
                dve.wait_ge(sem("hi_ready"), c.count(1))
            part = slice(half * CH // 2, (half + 1) * CH // 2)
            m = dve.tensor_tensor(w_lo[:, c.slot, part], w_raw[:, c.slot, part],
                                  w_hi[:, c.slot, part].bitcast(F32), ALU.subtract)
            if half:
                m.then_inc(sem("lo_ready"), 1)

        def split_lo(dve, c, cols=CH):
            dve.wait_ge(sem("hi_ready"), c.count(1))
            dve.tensor_tensor(w_lo[:, c.slot, 0:cols], w_raw[:, c.slot, 0:cols],
                              w_hi[:, c.slot, 0:cols].bitcast(F32), ALU.subtract).then_inc(
                sem("lo_ready"), 1)

        def t_products(pe, c, k_from=0, k_to=KT, width=P, free=None):
            if k_from == 0:
                pe.wait_ge(sem("lo_ready"), c.count(1))
                if free is not None:
                    pe.wait_ge(*free)
            out = bank[c.slot][0:width, :]
            for k in range(k_from, k_to):
                wh = w_hi[:, c.slot, k * width:(k + 1) * width]
                wl = w_lo[:, c.slot, k * width:(k + 1) * width]
                pe.matmul(out, wh, x_hi[:, k, :], start=(k == 0), stop=False)
                pe.matmul(out, wh, x_lo[:, k, :], start=False, stop=False)
                m = pe.matmul(out, wl, x_hi[:, k, :], start=False, stop=(k == KT - 1))
            if k_to == KT:
                m.then_inc(sem("chunk_done"), 1)

        def tile_done(eng, c, block, t):
            if t < NT - 1:
                eng.wait_ge(sem("tile_done"), block * (NT - 1) + (t + 1))
            else:
                eng.wait_ge(sem("chunk_done"), c.count(1))

        def n_products(pe, c, q, place=None, free=None, tiles=range(NT)):
            place = q if place is None else place
            pe.wait_ge(sem("lo_ready"), c.count(1))
            for t in tiles:
                if place == 0 and free is not None:
                    pe.wait_ge(*free(t))
                for k in range(4):
                    kt = 4 * q + k
                    xh, xl = x_hi[:, kt, ts(t, P)], x_lo[:, kt, ts(t, P)]
                    wh = w_hi[:, c.slot, k * 512:(k + 1) * 512]
                    wl = w_lo[:, c.slot, k * 512:(k + 1) * 512]
                    pe.matmul(bank[t][:, :], xh, wh, start=(place == 0 and k == 0), stop=False)
                    pe.matmul(bank[t][:, :], xh, wl, start=False, stop=False)
                    m = pe.matmul(bank[t][:, :], xl, wh, start=False, stop=(place == 3 and k == 3))
                if t == NT - 1:
                    m.then_inc(sem("chunk_done"), 1)
                elif place == 3:
                    m.then_inc(sem("tile_done"), 1)

        def passed(eng, name):
            eng.sem_inc(sem(name), 1)

        def rstd(act, out, ssq, scale, steps, count, bias=0.0):
            act.activation(out, ssq, ACT.Ln, scale=scale, bias=eps_col).then_inc(sem(steps), 1)
            act.wait_ge(sem(steps), count)
            return act.activation(out, out, ACT.Exp, scale=-0.5, bias=bias)

        def norm_stats_act(act, lay):
            if lay == 0:
                for t in range(NT):
                    act.wait_ge(sem(f"x_loaded{t}"), 16)
                    if t:
                        act.wait_ge(sem("rows_ssq"), t)
                    act.activation(square_out, rows[:, t, :], ACT.Square,
                                   accum_out=stat[:, t:t + 1]).then_inc(sem("rows_ssq"), 1)
                act.wait_ge(sem("rows_ssq"), NT)
            else:
                act.wait_ge(sem("ssq_summed"), 2)
            rstd(act, stat[:, 4:8], stat[:, 0:4], 1.0 / DM, "ln_done", 3 * lay + 1).then_inc(
                sem("rows_rstd"), 1)

        def norm_turn_act(act, lay, gain, tiles=range(KT)):
            for k in tiles:
                act.wait_ge(sem("rows_turned"), KT * lay + k + 1)
                act.activation(x_hi[:, k, :], bank[4 + k % 4][:, :], ACT.Copy,
                               scale=vcol(gain, k)).then_inc(sem("x_hi_ready"), 1)

        def block_squares(act, b):
            for t in range(NT):
                act.wait_ge(sem("block_summed"), 4 * b + t + 1)
                act.wait_ge(sem("rows_ssq"), NT + 4 * b + t)
                act.activation(square_out[:, 0:512], rows[:, t, b * 512:(b + 1) * 512], ACT.Square,
                               accum_out=ssq_parts[:, 4 * b + t:4 * b + t + 1]).then_inc(
                    sem("rows_ssq"), 1)

        def norm_rows_dve(dve, lay):
            if lay == 1:
                dve.wait_ge(sem("rows_ssq"), NT + 16)
                dve.tensor_tensor(ssq_parts[:, 0:8], ssq_parts[:, 0:8], ssq_parts[:, 8:16],
                                  ALU.add).then_inc(sem("ssq_summed"), 1)
                dve.wait_ge(sem("ssq_summed"), 1)
                dve.tensor_tensor(stat[:, 0:4], ssq_parts[:, 0:4], ssq_parts[:, 4:8],
                                  ALU.add).then_inc(sem("ssq_summed"), 1)
            else:
                dve.wait_ge(sem("small_loaded"), 16 * 11)
            dve.wait_ge(sem("rows_rstd"), lay + 1)
            for t in range(NT):
                dve.tensor_scalar(diag[:, t, :], ident, stat[:, 4 + t:5 + t], None,
                                  ALU.mult).then_inc(sem("diag_ready"), 1)

        def norm_turn_dve(dve, lay, gain, tiles=range(KT)):
            for k in tiles:
                dve.wait_ge(sem("x_hi_ready"), KT * lay + k + 1)
                dve.scalar_tensor_tensor(out=x_lo[:, k, :], in0=bank[4 + k % 4][:, :],
                                         scalar=vcol(gain, k), in1=x_hi[:, k, :].bitcast(F32),
                                         op0=ALU.mult, op1=ALU.subtract).then_inc(sem("x_lo_ready"), 1)

        def norm_pe(pe, lay):
            pe.wait_ge(sem("diag_ready"), NT * lay + NT)
            for k in range(KT):
                if k >= 4:
                    pe.wait_ge(sem("x_lo_ready"), KT * lay + k - 3)
                for t in range(NT):
                    m = pe.matmul(bank[4 + k % 4][:, ts(t, P)], rows[:, t, ts(k, P)], diag[:, t, :],
                                  start=True, stop=True)
                m.then_inc(sem("rows_turned"), 1)
            pe.wait_ge(sem("x_lo_ready"), KT * lay + KT)

        QUADS = {"out0": (0, 2, 1, 3), "out1a": (0, 1, 2, 3), "out1b": (0, 1, 2, 3)}
        PHASE = {"out0": 0, "out1a": 1, "out1b": 2}
        OUTS = {"out0": (N_OUT0, y0, 0, A["ab_w_out"], A["x"]),
                "out1a": (N_OUT1A, y1, 0, A["dn_w_out"], h_mid),
                "out1b": (N_OUT1B, y1, KT, A["dn_w_out"], None)}

        def out_sync(sp, tag):
            base, _, first, w, _ = OUTS[tag]
            with sp.Fori(0, 4) as b:
                for place, q in enumerate(QUADS[tag]):
                    load_chunk(sp, Chunk(base + place, b, 4),
                               w[(first + 4 * q) * P:(first + 4 * q + 4) * P, ds(b * 512, 512)], kts=4)

        def out_pool(eng, tag):
            res = OUTS[tag][4]
            for b in range(4):
                blk = slice(b * 512, (b + 1) * 512)
                if res is not None:
                    if b >= 2:
                        eng.wait_ge(sem("block_summed"), 16 * PHASE[tag] + 4 * (b - 1))
                    eng.dma_start(resid[:, b % 2], res[:, blk].rearrange(
                        "(t p) n -> p t n", p=P)).then_inc(sem(f"resid_loaded{b % 2}"), 16)
                if tag == "out0" and b >= 1 or tag == "out1b":
                    d = b - 1 if tag == "out0" else b
                    store_block(eng, tag, d)
            if tag == "out0":
                store_block(eng, tag, 3)

        def store_block(eng, tag, b):
            dst, done = (h_mid, "h_mid_stored") if tag == "out0" else (A["out"], "out_stored")
            blk = slice(b * 512, (b + 1) * 512)
            if tag == "out1b" and b == 3:
                for t in range(NT):
                    eng.wait_ge(sem("block_summed"), 16 * PHASE[tag] + 4 * b + t + 1)
                    eng.dma_start(dst[ts(t, P), blk], rows[:, t, blk]).then_inc(sem(done), 16)
                return
            eng.wait_ge(sem("block_summed"), 16 * PHASE[tag] + 4 * (b + 1))
            eng.dma_start(dst[:, blk].rearrange("(t p) n -> p t n", p=P),
                          rows[:, :, blk]).then_inc(sem(done), 16)

        def y_load(act, tag, place):
            _, src, first, _, _ = OUTS[tag]
            q = QUADS[tag][place]
            for name, count in {"out0": ((f"y0_stored{q // 2 * 2}", 32 + q % 2 * 32),
                                         (f"y0_stored{q // 2 * 2 + 1}", 32 + q % 2 * 32)),
                                "out1a": (("y1_stored0", 16 * 8), ("y1_stored1", 16 * 8)),
                                "out1b": (("y1_stored0", 16 * H_QK), ("y1_stored1", 16 * H_QK))}[tag]:
                act.wait_ge(sem(name), count)
            act.dma_start(x_lo[:, 4 * q:4 * q + 4, :].bitcast(F32),
                          src[first + 4 * q:first + 4 * q + 4].rearrange("k p s -> p k s")).then_inc(
                sem(f"y_loaded{q}"), 16)

        def y_hi(act, tag, place):
            q = QUADS[tag][place]
            act.wait_ge(sem(f"y_loaded{q}"), 16 * PHASE[tag] + 16)
            act.activation(x_hi[:, 4 * q:4 * q + 4, :], x_lo[:, 4 * q:4 * q + 4, :].bitcast(F32),
                           ACT.Copy).then_inc(sem("y_hi_ready"), 1)

        def y_lo(dve, tag, place):
            q = QUADS[tag][place]
            dve.wait_ge(sem("y_hi_ready"), 4 * PHASE[tag] + place + 1)
            dve.tensor_tensor(x_lo[:, 4 * q:4 * q + 4, :], x_lo[:, 4 * q:4 * q + 4, :].bitcast(F32),
                              x_hi[:, 4 * q:4 * q + 4, :].bitcast(F32), ALU.subtract).then_inc(
                sem("y_lo_ready"), 1)

        def out_act(act, tag):
            base = OUTS[tag][0]
            if tag == "out0":
                act.wait_ge(sem("chunk_done"), base)
                y_load(act, tag, 0)
                y_load(act, tag, 1)
                y_hi(act, tag, 0)
                y_hi(act, tag, 1)
                y_load(act, tag, 2)
                y_load(act, tag, 3)
                y_hi(act, tag, 2)
                y_hi(act, tag, 3)
            for n in range(base + 2, base + 18):
                if n < N_END:
                    split_hi(act, Chunk(n), cols=cols_of(n))
                if tag == "out0" and (n - base) % 4 == 0:
                    block_squares(act, (n - base) // 4 - 1)
                if tag == "out1a":
                    place = n - (base + 14)
                    if place > 0:
                        y_hi(act, "out1b", place - 1)
                    if place >= 0:
                        y_load(act, "out1b", place)
            if tag == "out1a":
                y_hi(act, "out1b", 3)

        def out_dve(dve, tag):
            base, _, _, _, res = OUTS[tag]
            if tag == "out0":
                for place in range(4):
                    y_lo(dve, tag, place)
            for b in range(4):
                for q in range(3):
                    if tag == "out1a" and b == 3 and q:
                        y_lo(dve, "out1b", q - 1)
                    if base + 4 * b + q + 2 < N_END:
                        split_lo(dve, Chunk(base + 4 * b + q + 2), cols=cols_of(base + 4 * b + q + 2))
                if res is not None:
                    dve.wait_ge(sem(f"resid_loaded{b % 2}"), 32 * PHASE[tag] + 16 * (b // 2 + 1))
                for t in range(NT):
                    tile_done(dve, Chunk(base + 4 * b + 3), 4 * (1 + PHASE[tag]) + b, t)
                    r = rows[:, t, b * 512:(b + 1) * 512]
                    dve.tensor_tensor(r, bank[t][:, :], r if res is None else resid[:, b % 2, t, :],
                                      ALU.add).then_inc(sem("block_summed"), 1)
                if base + 4 * b + 5 < N_END:
                    split_lo(dve, Chunk(base + 4 * b + 5), cols=cols_of(base + 4 * b + 5))
            if tag == "out1a":
                y_lo(dve, "out1b", 2)
                y_lo(dve, "out1b", 3)

        def out_pe(pe, tag, part="all"):
            base = OUTS[tag][0]
            first_free = {"out0": None,
                          "out1a": lambda t: (sem("y1_made"), 2 * H_QK - 1) if t == 3 else
                                             (sem("z_ready"), 2 * H_QK),
                          "out1b": lambda t: (sem("block_summed"), 16 * PHASE[tag] + t - 3)}[tag]
            for place, q in enumerate(QUADS[tag]):
                if part == "start" and place:
                    return
                tiles = {"all": range(NT), "start": range(3), "rest": range(3, NT)}[part if place == 0 else "all"]
                pe.wait_ge(sem("y_lo_ready"), 4 * PHASE[tag] + place + 1)
                n_products(pe, Chunk(base + place), q, place, free=first_free, tiles=tiles)
            with pe.Fori(1, 4) as b:
                for place, q in enumerate(QUADS[tag]):
                    n_products(pe, Chunk(base + place, b, 4), q, place,
                               free=lambda t: (sem("block_summed"), b * 4 + (16 * PHASE[tag] + t - 3)))

        def cols_of(n):
            return {N_KI: KT * 72, N_BA: KT * 64}.get(n, CH)


        IDX_T = (1, 2, 3)
        ioff = {1: 0, 2: 256, 3: 640}

        def pre_pe(pe):
            pe.wait_ge(sem("small_loaded"), 16 * 11)
            pe.transpose(bank[0][:, 0:V_ROWS], rows_in[0:V_ROWS, :], ident[0:V_ROWS, 0:V_ROWS]).then_inc(
                sem("gains_turned"), 1)
            for j in range(2):
                m = pe.transpose(bank[1][:, ts(j, P)], y_stage[:, 8 + j, 0:P], ident)
            m.then_inc(sem("gains_turned"), 1)
            norm_pe(pe, 0)
            pe.wait_ge(sem("vec_ready"), 2)
            t_products(pe, Chunk(0))
            t_products(pe, Chunk(1))
            t_products(pe, Chunk(N_KI), width=72, free=(sem("l0_drained"), 1))
            pe.wait_ge(sem("c_raw"), 2)
            for t in range(NT):
                for j in range(2):
                    m = pe.transpose(bank[2 + t // 2][:, (t % 2) * D_C + j * P:(t % 2) * D_C + (j + 1) * P],
                                     c_t[:, j, ts(t, P)], ident)
            m.then_inc(sem("latent_steps"), 1)
            t_products(pe, Chunk(3), free=(sem("l0_drained"), 2))
            pe.wait_ge(sem("wi_raw"), 1)
            for t in range(NT):
                m = pe.transpose(bank[4][:, t * H_I:(t + 1) * H_I], wi_t[0:H_I, ts(t, P)], ident[0:H_I, 0:H_I])
            m.then_inc(sem("latent_steps"), 1)
            pe.wait_ge(sem("c_n_ready"), NT)
            for j in range(2):
                for t in range(NT):
                    m = pe.transpose(bank[2 + j][:, ts(t, P)], c_n[:, t, ts(j, P)], ident)
            m.then_inc(sem("latent_steps"), 1)

            def index_head(h):
                pe.wait_ge(sem("qi_ready"), h // 2 + 1)
                if h >= 1:
                    pe.wait_ge(sem("relu_ready"), 3 * h)
                r = slice(64 * (h % 2), 64 * (h % 2) + 64)
                for t in IDX_T:
                    m = pe.matmul(bank[4 + t][:, 0:wid[t]], qi_t[r, (h // 2) % 2, ts(t, P)],
                                  ki_t[r, 0:wid[t]], start=True, stop=True)
                m.then_inc(sem("index_done"), 1)

            pe.wait_ge(sem("ki_ready"), 2)
            t_products(pe, Chunk(4), 0, 8, free=(sem("l0_drained"), 3))
            index_head(0)
            t_products(pe, Chunk(4), 8, KT)
            index_head(1)
            pe.wait_ge(sem("ct_ready"), 2)
            pe.wait_ge(sem("wi_n_ready"), 1)
            for t in range(NT):
                for j in range(2):
                    m = pe.matmul(bank[4][:, ts(t, P)], c_t[:, j, ts(t, P)], w_uk[:, j, :],
                                  start=(j == 0), stop=(j == 1))
            m.then_inc(sem("latent_steps"), 1)
            t_products(pe, Chunk(5), 0, 8, free=(sem("l0_drained"), 4))
            index_head(2)
            t_products(pe, Chunk(5), 8, KT)
            index_head(3)
            pe.wait_ge(sem("k_n_ready"), NT)
            for t in range(NT):
                m = pe.transpose(bank[2][:, ts(t, P)], k_n[:, t, :], ident)
            m.then_inc(sem("latent_steps"), 1)
            t_products(pe, Chunk(6), 0, 8, free=(sem("l0_drained"), 5))
            index_head(4)
            t_products(pe, Chunk(6), 8, KT)
            for h in (5, 6, 7):
                index_head(h)
            pe.wait_ge(sem("key_ready"), 1)
            pe.wait_ge(sem("l0_drained"), 7)
            with pe.Fori(0, 4) as b:
                for q in range(4):
                    n_products(pe, Chunk(N_QKVB + q, b, 4), q,
                               free=lambda t: (sem("l0_drained"), b * 4 + (t + 4)))

        def pre_sync(sp):
            for t in range(NT):
                sp.dma_start(rows[:, t, :], A["x"][ts(t, P), :]).then_inc(sem(f"x_loaded{t}"), 16)
            for n in range(7):
                if n < 2:
                    load_chunk(sp, Chunk(n), A["ab_w_in"][:, C_C + n * P:C_C + (n + 1) * P])
                elif n == N_KI:
                    load_chunk(sp, Chunk(n), A["ab_w_in"][:, C_KI:C_KI + 72], cols=KT * 72)
                else:
                    a = C_QI + (n - N_QI) * P
                    load_chunk(sp, Chunk(n), A["ab_w_in"][:, a:a + P])
            with sp.Fori(0, 4) as b:
                for q in range(4):
                    load_chunk(sp, Chunk(N_QKVB + q, b, 4),
                               A["ab_w_in"][q * 512:(q + 1) * 512, ds(b * 512 + C_QKVB, 512)], kts=4)

        def pre_act(act):
            act.dma_start(k0, A["k0"]).then_inc(sem("small_loaded"), 16)
            for name, (a, n) in _V.items():
                act.dma_start(rows_in[a:a + n, :], A[name]).then_inc(sem("small_loaded"), 16)
            for j in range(2):
                act.dma_start(y_stage[:, 8 + j, 0:P], A["dn_conv"][ts(j, P), :]).then_inc(sem("small_loaded"), 16)
            act.dma_start(w_uk, A["ab_w_uk"].rearrange("(j p) d -> p j d", p=P)).then_inc(sem("small_loaded"), 16)
            act.wait_ge(sem("eps_ready"), 3)
            norm_stats_act(act, 0)
            act.wait_ge(sem("gains_turned"), 1)
            act.activation(vec, bank[0][:, 0:V_ROWS], ACT.Copy).then_inc(sem("vec_ready"), 1)
            act.wait_ge(sem("gains_turned"), 2)
            act.activation(taps, bank[1][:, 0:256], ACT.Copy).then_inc(sem("vec_ready"), 1)
            act.wait_ge(sem("vec_ready"), 2)
            norm_turn_act(act, 0, "ab_norm", range(12))
            split_hi(act, Chunk(0))
            norm_turn_act(act, 0, "ab_norm", range(12, KT))
            split_hi(act, Chunk(1))

            def drain(n, out, part=slice(0, P), then=None, at=None):
                act.wait_ge(sem("chunk_done"), n + 1)
                return act.activation(out, bank[n % 2][part, :], ACT.Copy)

            def relu(h):
                act.wait_ge(sem("index_done"), h + 1)
                if h >= 2:
                    act.wait_ge(sem("score_added"), 3 * (h - 1))
                for t in IDX_T:
                    act.activation(relu_s[:, h % 2, ioff[t]:ioff[t] + wid[t]], bank[4 + t][:, 0:wid[t]],
                                   ACT.Relu).then_inc(sem("relu_ready"), 1)

            for n in (0, 1):
                split_hi(act, Chunk(n + 2), cols=cols_of(n + 2))
                m = drain(n, c_t[:, n, :])
                m.then_inc(sem("c_raw"), 1)
                act.wait_ge(sem("c_raw"), n + 1)
                act.sem_inc(sem("l0_drained"), 1)
            split_hi(act, Chunk(4))
            act.wait_ge(sem("chunk_done"), 3)
            for half in range(2):
                act.activation(ki_t[64 * half:64 * half + 64, :], bank[0][0:64, :], ACT.Copy).then_inc(
                    sem("ki_ready"), 1)
            act.activation(wi_t[0:H_I, :], bank[0][64:64 + H_I, :], ACT.Copy,
                           scale=H_I ** -0.5 * D_I ** -0.5).then_inc(sem("wi_raw"), 1)
            act.wait_ge(sem("wi_raw"), 1)
            act.wait_ge(sem("ki_ready"), 2)
            act.sem_inc(sem("l0_drained"), 1)
            act.wait_ge(sem("latent_steps"), 1)
            for t in range(NT):
                src = bank[2 + t // 2][:, (t % 2) * D_C:(t % 2 + 1) * D_C]
                act.activation(c_n[:, t, :], src, ACT.Square,
                               accum_out=stat[:, 8 + t:9 + t]).then_inc(sem("small_ssq"), 1)
            act.wait_ge(sem("small_ssq"), NT)
            rstd(act, stat[:, 12:16], stat[:, 8:12], 1.0 / D_C, "ln_done", 2).then_inc(sem("small_rstd"), 1)
            act.wait_ge(sem("small_rstd"), 1)
            for t in range(NT):
                act.activation(c_n[:, t, :], bank[2 + t // 2][:, (t % 2) * D_C:(t % 2 + 1) * D_C], ACT.Copy,
                               scale=stat[:, 12 + t:13 + t]).then_inc(sem("c_n_ready"), 1)

            def drain_qi(j):
                n = N_QI + j
                if j >= 2:
                    act.wait_ge(sem("index_done"), 2 * (j - 1))
                drain(n, qi_t[:, j % 2, :]).then_inc(sem("qi_ready"), 1)
                act.wait_ge(sem("qi_ready"), j + 1)
                act.sem_inc(sem("l0_drained"), 1)

            split_hi(act, Chunk(5))
            drain_qi(0)
            act.wait_ge(sem("latent_steps"), 2)
            act.activation(wi_n, bank[4][:, 0:NT * H_I].rearrange("p (t h) -> p t h", t=NT),
                           ACT.Copy).then_inc(sem("wi_n_ready"), 1)
            act.wait_ge(sem("latent_steps"), 3)
            for j in range(2):
                act.activation(c_t[:, j, :], bank[2 + j][:, :], ACT.Copy,
                               scale=vcol("ab_kv_norm", j)).then_inc(sem("ct_ready"), 1)
            relu(0)
            split_hi(act, Chunk(6))
            drain_qi(1)
            relu(1)
            act.wait_ge(sem("latent_steps"), 4)
            for t in range(NT):
                act.activation(k_n[:, t, :], bank[4][:, ts(t, P)], ACT.Square,
                               accum_out=stat[:, t:t + 1]).then_inc(sem("small_ssq"), 1)
            act.wait_ge(sem("small_ssq"), 2 * NT)
            rstd(act, stat[:, 4:8], stat[:, 0:4], 1.0 / P, "ln_done", 3).then_inc(sem("small_rstd"), 1)
            act.wait_ge(sem("small_rstd"), 2)
            for t in range(NT):
                act.activation(k_n[:, t, :], bank[4][:, ts(t, P)], ACT.Copy,
                               scale=stat[:, 4 + t:5 + t]).then_inc(sem("k_n_ready"), 1)
            relu(2)
            split_hi(act, Chunk(7))
            drain_qi(2)
            relu(3)
            act.wait_ge(sem("latent_steps"), 5)
            act.wait_ge(sem("kq_gain_ready"), 1)
            act.activation(key_t, bank[2][:, :], ACT.Copy, scale=kq_gain).then_inc(sem("key_ready"), 1)
            relu(4)
            split_hi(act, Chunk(8))
            drain_qi(3)
            for h in (5, 6, 7):
                relu(h)
            with act.Fori(0, 4) as b:
                for q in range(4):
                    c = Chunk(N_QKVB + q, b, 4)
                    if q == 3:
                        for t in range(NT):
                            tile_done(act, c, b, t)
                            act.activation(qkvb[:, t, ds(b * 512, 512)], bank[t][:, :],
                                           ACT.Copy).then_inc(sem("l0_drained"), 1)
                    split_hi(act, c.plus(2))

        def pre_dve(dve):
            dve.memset(eps_col, EPS).then_inc(sem("eps_ready"), 1)
            dve.memset(one_col, 1.0).then_inc(sem("eps_ready"), 1)
            dve.memset(ln_col, -0.5 * math.log(P)).then_inc(sem("eps_ready"), 1)
            dve.wait_ge(sem("eps_ready"), 3)
            norm_rows_dve(dve, 0)
            dve.wait_ge(sem("vec_ready"), 2)
            dve.tensor_tensor(kq_gain, vcol("ab_q_norm"), vcol("ab_k_norm"), ALU.mult).then_inc(
                sem("kq_gain_ready"), 1)
            norm_turn_dve(dve, 0, "ab_norm", range(12))
            split_lo(dve, Chunk(0))
            norm_turn_dve(dve, 0, "ab_norm", range(12, KT))
            split_lo(dve, Chunk(1))

            def add_scores(h):
                if h == 0:
                    dve.wait_ge(sem("wi_n_ready"), 1)
                for j, t in enumerate(IDX_T):
                    dve.wait_ge(sem("relu_ready"), 3 * h + j + 1)
                    r = relu_s[:, h % 2, ioff[t]:ioff[t] + wid[t]]
                    sc = bias[:, off[t]:off[t] + wid[t]]
                    w = wi_n[:, t, h:h + 1]
                    if h == 0:
                        dve.tensor_scalar(sc, r, w, None, ALU.mult).then_inc(sem("score_added"), 1)
                    else:
                        dve.wait_ge(sem("score_added"), 3 * (h - 1) + j + 1)
                        dve.scalar_tensor_tensor(out=sc, in0=r, scalar=w, in1=sc, op0=ALU.mult,
                                                 op1=ALU.add).then_inc(sem("score_added"), 1)

            for n in (2, 3, 4, 5):
                split_lo(dve, Chunk(n), cols=cols_of(n))
            add_scores(0)
            split_lo(dve, Chunk(6))
            add_scores(1)
            add_scores(2)
            split_lo(dve, Chunk(7))
            add_scores(3)
            add_scores(4)
            split_lo(dve, Chunk(8))
            for h in (5, 6, 7):
                add_scores(h)
            for j, t in enumerate(IDX_T):
                dve.wait_ge(sem("score_added"), 3 * 7 + j + 1)
                d = bias[:, off[t] + t * P:off[t] + (t + 1) * P]
                dve.tensor_tensor(d, d, const("hide_low"), ALU.add).then_inc(sem("ranked"), 1)
            dve.tensor_copy(bias[:, 0:P], const("hide_low")).then_inc(sem("bias_ready"), 1)
            with dve.Fori(0, 4) as b:
                for q in range(4):
                    for j, t in enumerate(IDX_T):
                        dve.wait_ge(sem("ranked"), b * 24 + (6 * q + j + 1))
                        passed(dve, "dve_passed")
                        dve.max(top8[:, j, :], bias[:, off[t]:off[t] + wid[t]]).then_inc(sem("ranked"), 1)
                    for j, t in enumerate(IDX_T):
                        dve.wait_ge(sem("ranked"), b * 24 + (6 * q + j + 4))
                        sc = bias[:, off[t]:off[t] + wid[t]]
                        passed(dve, "dve_passed")
                        dve.match_replace(sc, top8[:, j, :], sc, TAKEN).then_inc(sem("ranked"), 1)
                    split_lo(dve, Chunk(N_QKVB + q + 2, b, 4))
            assert TOPK == 16 * 8
            for j, t in enumerate(IDX_T):
                dve.wait_ge(sem("ranked"), 3 + 96)
                sc = bias[:, off[t]:off[t] + wid[t]]
                dve.tensor_scalar(sc, sc, -2.0e38, HIDE, ALU.is_gt, ALU.mult).then_inc(sem("bias_ready"), 1)
            dve.wait_ge(sem("bias_ready"), 4)

        def hc(i, k):
            return Chunk(N_HEADS + k, i, 6)

        def n(i, per, k):
            return per * i + k if isinstance(i, int) else i * per + k

        def earlier(eng, name, i, per):
            if not (isinstance(i, int) and i == 0):
                eng.wait_ge(sem(name), n(i, per, 0))

        def heads_sync(sp):
            heads_sync_one(sp, 0)
            with sp.Fori(1, 4) as i:
                heads_sync_one(sp, i)

        def heads_sync_one(sp, i):
            cols = [i * 256 + C_QA, i * 256 + C_GATE, i * 256 + C_QA + P, i * 256 + C_GATE + P,
                    i * 256 + C_GATE + 1024, i * 256 + C_GATE + 1024 + P]
            for k in range(6):
                load_chunk(sp, hc(i, k), A["ab_w_in"][:, ds(cols[k], P)])
                if k == 2:
                    earlier(sp, "uv_done", i, 2)
                    for e in range(2):
                        sp.dma_start(w_uv[:, e], A["ab_w_uv"][ds(i * 512 + e * 256, 256), :].rearrange(
                            "(j p) d -> p j d", p=P)).then_inc(sem(f"uv_loaded{e}"), 16)

        def heads_pe(pe):
            heads_pe_one(pe, 0)
            with pe.Fori(1, 4) as i:
                heads_pe_one(pe, i)

        def heads_pe_one(pe, i):
            def prod(k, a=0, b=KT):
                c = hc(i, k)
                t_products(pe, c, a, b, free=(sem("l0_drained"), c.count(-1)))

            def logits(e, ssq_bank):
                pe.wait_ge(sem("q_sq_ready"), n(i, 2, e + 1))
                for t in range(NT):
                    m = pe.matmul(bank[ssq_bank][:, t:t + 1], q_sq[:, ts(t, P)], ones[:, 0:1],
                                  start=True, stop=True)
                m.then_inc(sem("q_ssq_done"), 1)
                for t in range(NT):
                    m = pe.matmul(bank[4 + t][:, 0:wid[t]], q_t[:, ts(t, P)], key_t[:, 0:wid[t]],
                                  start=True, stop=True)
                m.then_inc(sem("logits_done"), 1)

            def turn_prob(e):
                pe.wait_ge(sem("prob_ready"), n(i, 8, 4 * e + 4))
                for s in range(NT):
                    for t in range(s, NT):
                        m = pe.transpose(bank[4 + s][:, ts(t, P)],
                                         prob[:, off[t] + s * P:off[t] + (s + 1) * P], ident)
                    m.then_inc(sem("prob_turned"), 1)

            def latent(e):
                pe.wait_ge(sem("prob_t_act"), n(i, 4, 2 * e + 2))
                pe.wait_ge(sem("prob_t_dve"), n(i, 4, 2 * e + 2))
                for j in range(2):
                    for s in range(NT):
                        w = SEQ - s * P
                        m = pe.matmul(bank[4 + j][:, s * P:SEQ], c_n[:, s, ts(j, P)],
                                      prob_t[:, toff[s]:toff[s] + w], start=(s == 0), stop=(s == NT - 1))
                    m.then_inc(sem("lat_done"), 1)

            def up(e, b):
                pe.wait_ge(sem("lat_ready"), n(i, 4, 2 * e + 2))
                pe.wait_ge(sem(f"uv_loaded{e}"), n(i, 16, 16))
                for j in range(2):
                    m = pe.matmul(bank[b][:, :], w_uv[:, e, j, :], lat_t[:, j, :], start=(j == 0),
                                  stop=(j == 1))
                m.then_inc(sem("uv_done"), 1)

            prod(0)
            pe.wait_ge(sem("rot_ready"), n(i, 2, 2))
            earlier(pe, "ret_n_ready", i, 4)
            for j in range(2):
                for t in range(NT):
                    m = pe.transpose(bank[2 + j][:, ts(t, P)], rot[:, j, t, :], ident)
                m.then_inc(sem("rot_turned"), 1)
            prod(1, 0, 8)
            earlier(pe, "y_made", i, 4)
            pe.wait_ge(sem("rot_t_ready"), n(i, 2, 2))
            logits(0, 3)
            for t in range(NT):
                m = pe.matmul(bank[2][:, ts(t, P)], rot_t[:, 1, ts(t, P)], rot_t[:, 0, ts(t, P)],
                              start=True, stop=True)
            m.then_inc(sem("inner_done"), 1)
            prod(1, 8, KT)
            prod(2, 0, 13)
            turn_prob(0)
            pe.wait_ge(sem("inner_ready"), n(i, 1, 1))
            pe.wait_ge(sem("q_scale_ready"), n(i, 2, 1))
            for t in range(3):
                o = bank[2 + t // 2][:, (t % 2) * DV_B:(t % 2 + 1) * DV_B]
                m = pe.matmul(o, k_dec[:, t, :], qkvb[:, t, ds(i * DV_B + 1024, DV_B)],
                              start=True, stop=True)
            m.then_inc(sem("kv_done"), 1)
            prod(2, 13, KT)
            latent(0)
            prod(3, 0, 8)
            pe.wait_ge(sem("ret_s_ready"), n(i, 3, 3))
            up(0, 3)
            logits(1, 2)
            prod(3, 8, KT)
            prod(4, 0, 13)
            turn_prob(1)
            pe.wait_ge(sem("q_scale_ready"), n(i, 2, 2))
            pe.wait_ge(sem("y_made"), n(i, 4, 1))
            for t in range(NT):
                o = bank[2 + t // 2][:, (t % 2) * DV_B:(t % 2 + 1) * DV_B]
                m = pe.matmul(o, inner_t[:, ts(t, P)], qkvb[:, t, ds(i * DV_B + 1024, DV_B)],
                              start=True, stop=(t == 0))
                if t:
                    m = pe.matmul(o, rot_t[:, 0, ts(t, P)], ret_s[:, t - 1, :], start=False, stop=True)
            m.then_inc(sem("ret_out_done"), 1)
            prod(4, 13, KT)
            latent(1)
            prod(5, 0, 8)
            up(1, 6)
            pe.wait_ge(sem("ret_n_ready"), n(i, 4, 4))
            for j in range(2):
                for t in range(NT):
                    m = pe.transpose(bank[4 + j][:, ts(t, P)], ret_n[:, t, ts(j, P)], ident)
                m.then_inc(sem("ret_turned"), 1)
            prod(5, 8, KT)

        def heads_act(act):
            heads_act_one(act, 0)
            with act.Fori(1, 4) as i:
                heads_act_one(act, i)

        def heads_act_one(act, i):
            def after(k, out, func):
                split_hi(act, hc(i, k + 2))
                act.wait_ge(sem("chunk_done"), hc(i, k).count(1))
                act.activation(out, bank[hc(i, k).slot][:, :], func).then_inc(sem("l0_drained"), 1)

            def after_query(e):
                if e == 0:
                    earlier(act, "logits_done", i, 2)
                else:
                    act.wait_ge(sem("logits_done"), n(i, 2, 1))
                after(2 * e, q_t, ACT.Copy)
                act.wait_ge(sem("l0_drained"), hc(i, 2 * e).count(1))
                act.activation(q_sq, q_t, ACT.Square).then_inc(sem("q_sq_ready"), 1)

            def scale(e, b):
                act.wait_ge(sem("q_ssq_done"), n(i, 2, e + 1))
                rstd(act, soft[:, 0:4], bank[b][:, 0:4], 1.0 / P, "head_ln_done", n(i, 3, e + 1),
                     bias=ln_col).then_inc(sem("q_scale_ready"), 1)

            def exps(e):
                act.wait_ge(sem("soft_bias_ready"), n(i, 2, e + 1))
                for t in range(NT):
                    p = prob[:, off[t]:off[t] + wid[t]]
                    act.activation(p, p, ACT.Exp, scale=soft[:, t:t + 1], bias=soft[:, 8 + t:9 + t],
                                   accum_out=soft[:, 12 + t:13 + t]).then_inc(sem("exp_done"), 1)

            def drain_prob_t(e):
                for s in range(2):
                    act.wait_ge(sem("prob_turned"), n(i, 8, 4 * e + s + 1))
                    act.activation(prob_t[:, toff[s]:toff[s] + SEQ - s * P], bank[4 + s][:, s * P:SEQ],
                                   ACT.Copy).then_inc(sem("prob_t_act"), 1)

            def drain_latent(e):
                for j in range(2):
                    act.wait_ge(sem("lat_done"), n(i, 4, 2 * e + j + 1))
                    act.activation(lat_t[:, j, :], bank[4 + j][:, :], ACT.Copy,
                                   scale=vcol("ab_kv_norm", j)).then_inc(sem("lat_ready"), 1)

            after_query(0)
            earlier(act, "ret_out_done", i, 1)
            for j in range(2):
                act.wait_ge(sem("rot_turned"), n(i, 2, j + 1))
                act.activation(rot_t[:, j, :], bank[2 + j][:, :], ACT.Copy).then_inc(sem("rot_t_ready"), 1)
            scale(0, 3)
            earlier(act, "y0_stored0", i, 16)
            after(1, gate[:, 0, :], ACT.Silu)
            exps(0)
            drain_prob_t(0)
            after_query(1)
            drain_latent(0)
            scale(1, 2)
            earlier(act, "y0_stored1", i, 16)
            after(3, gate[:, 1, :], ACT.Silu)
            exps(1)
            drain_prob_t(1)
            act.wait_ge(sem("ret_out_done"), n(i, 1, 1))
            earlier(act, "ret_turned", i, 2)
            for t in range(NT):
                act.activation(ret_n[:, t, :], bank[2 + t // 2][:, (t % 2) * DV_B:(t % 2 + 1) * DV_B],
                               ACT.Square, accum_out=stat[:, t:t + 1]).then_inc(sem("ret_ssq"), 1)
            earlier(act, "y0_stored2", i, 16)
            after(4, gate[:, 2, :], ACT.Silu)
            act.wait_ge(sem("ret_ms_ready"), n(i, 1, 1))
            rstd(act, stat[:, 4:8], stat[:, 4:8], 1.0, "head_ln_done", n(i, 3, 3)).then_inc(sem("ret_rstd"), 1)
            act.wait_ge(sem("ret_scale_ready"), n(i, 1, 1))
            for t in range(NT):
                act.activation(ret_n[:, t, :], bank[2 + t // 2][:, (t % 2) * DV_B:(t % 2 + 1) * DV_B],
                               ACT.Copy, scale=stat[:, 8 + t:9 + t]).then_inc(sem("ret_n_ready"), 1)
            drain_latent(1)
            earlier(act, "y0_stored3", i, 16)
            after(5, gate[:, 3, :], ACT.Silu)

        def heads_dve(dve):
            heads_dve_one(dve, 0)
            with dve.Fori(1, 4) as i:
                heads_dve_one(dve, i)

        def heads_dve_one(dve, i):
            def soft_max(e):
                dve.wait_ge(sem("logits_done"), n(i, 2, e + 1))
                dve.wait_ge(sem("prob_turned"), n(i, 8, 4 * e))
                passed(dve, "dve_passed")
                for t in range(NT):
                    w = wid[t]
                    dve.tensor_tensor_reduce(out=prob[:, off[t]:off[t] + w], in0=bank[4 + t][:, 0:w],
                                             in1=bias[:, off[t]:off[t] + w], scale=1.0, scalar=-3.0e38,
                                             op0=ALU.add, op1=ALU.max,
                                             accum_out=soft[:, 4 + t:5 + t]).then_inc(sem("max_done"), 1)
                dve.wait_ge(sem("max_done"), n(i, 8, 4 * e + 4))
                dve.wait_ge(sem("q_scale_ready"), n(i, 2, e + 1))
                dve.scalar_tensor_tensor(out=soft[:, 8:12], in0=soft[:, 4:8], scalar=-1.0,
                                         in1=soft[:, 0:4], op0=ALU.mult, op1=ALU.mult).then_inc(
                    sem("soft_bias_ready"), 1)

            def normalise(e):
                dve.wait_ge(sem("exp_done"), n(i, 8, 4 * e + 4))
                dve.reciprocal(soft[:, 16:20], soft[:, 12:16]).then_inc(sem("sum_inverted"), 1)
                dve.wait_ge(sem("sum_inverted"), n(i, 2, e + 1))
                for t in range(NT):
                    p = prob[:, off[t]:off[t] + wid[t]]
                    dve.tensor_scalar(p, p, soft[:, 16 + t:17 + t], None, ALU.mult).then_inc(
                        sem("prob_ready"), 1)

            def drain_prob_t(e):
                for s in (2, 3):
                    dve.wait_ge(sem("prob_turned"), n(i, 8, 4 * e + s + 1))
                    dve.tensor_copy(prob_t[:, toff[s]:toff[s] + SEQ - s * P],
                                    bank[4 + s][:, s * P:SEQ]).then_inc(sem("prob_t_dve"), 1)

            def gated(e, b):
                dve.wait_ge(sem("uv_done"), n(i, 2, e + 1))
                dve.wait_ge(sem("l0_drained"), hc(i, 2 * e + 1).count(1))
                dve.tensor_tensor(gate[:, e, :], bank[b][:, :], gate[:, e, :], ALU.mult).then_inc(
                    sem("y_made"), 1)

            dve.tensor_copy(ret_c, ret_tab[:, :, ds(i, 1)].rearrange("p a b -> p (a b)")).then_inc(
                sem("ret_c_ready"), 1)
            dve.wait_ge(sem("ret_c_ready"), n(i, 1, 1))
            dve.wait_ge(sem("rot_ready"), n(i, 2, 2))
            earlier(dve, "kv_done", i, 1)
            dve.tensor_scalar(k_dec, rot[:, 1], ret_c[:, 1:2], None, ALU.mult).then_inc(
                sem("k_dec_ready"), 1)
            split_lo(dve, hc(i, 2))
            soft_max(0)
            dve.wait_ge(sem("inner_done"), n(i, 1, 1))
            dve.scalar_tensor_tensor(out=by_tile(inner_t), in0=by_tile(bank[2][:, :]),
                                     scalar=ret_c[:, 0:1], in1=tiled(const("tri_up")), op0=ALU.mult,
                                     op1=ALU.mult).then_inc(sem("inner_ready"), 1)
            split_lo(dve, hc(i, 3))
            normalise(0)
            drain_prob_t(0)
            dve.wait_ge(sem("kv_done"), n(i, 1, 1))
            earlier(dve, "ret_out_done", i, 1)
            dve.tensor_copy(ret_s[:, 0, :], bank[2][:, 0:DV_B]).then_inc(sem("ret_s_ready"), 1)
            for s in (1, 2):
                dve.wait_ge(sem("ret_s_ready"), n(i, 3, s))
                dve.scalar_tensor_tensor(out=ret_s[:, s, :], in0=ret_s[:, s - 1, :],
                                         scalar=ret_c[:, 4:5],
                                         in1=bank[2 + s // 2][:, (s % 2) * DV_B:(s % 2 + 1) * DV_B],
                                         op0=ALU.mult, op1=ALU.add).then_inc(sem("ret_s_ready"), 1)
            split_lo(dve, hc(i, 4))
            gated(0, 3)
            soft_max(1)
            split_lo(dve, hc(i, 5))
            normalise(1)
            drain_prob_t(1)
            split_lo(dve, hc(i, 6))
            dve.wait_ge(sem("ret_ssq"), n(i, 4, 4))
            dve.tensor_scalar(stat[:, 4:8], stat[:, 0:4], ret_c[:, 2:3], None, ALU.mult).then_inc(
                sem("ret_ms_ready"), 1)
            dve.wait_ge(sem("ret_rstd"), n(i, 1, 1))
            dve.tensor_scalar(stat[:, 8:12], stat[:, 4:8], ret_c[:, 3:4], None, ALU.mult).then_inc(
                sem("ret_scale_ready"), 1)
            split_lo(dve, hc(i, 7))
            gated(1, 6)
            for j in range(2):
                dve.wait_ge(sem("ret_turned"), n(i, 2, j + 1))
                dve.wait_ge(sem("l0_drained"), hc(i, 4 + j).count(1))
                dve.scalar_tensor_tensor(out=gate[:, 2 + j, :], in0=bank[4 + j][:, :],
                                         scalar=vec[:, ds(i * 2 + _V["ab_ret_norm"][0] + j, 1)],
                                         in1=gate[:, 2 + j, :], op0=ALU.mult, op1=ALU.mult).then_inc(
                    sem("y_made"), 1)

        def heads_pool(eng):
            def rotate(i):
                if not (isinstance(i, int) and i == 0):
                    earlier(eng, "rot_turned", i, 2)
                    earlier(eng, "k_dec_ready", i, 1)
                    passed(eng, "pool_passed")
                cos = const("cos").rearrange("p (t d) -> p t d", t=NT)
                sin = const("sin").rearrange("p (t d) -> p t d", t=NT)
                step = [0]

                def done(m):
                    step[0] += 1
                    m.then_inc(sem("rot_step"), 1)
                    eng.wait_ge(sem("rot_step"), n(i, 12, step[0]))
                    passed(eng, "pool_passed")

                for j in range(2):
                    x1 = qkvb[:, :, ds(i * P + j * 512, 64)]
                    x2 = qkvb[:, :, ds(i * P + j * 512 + 64, 64)]
                    lo, hi = rot[:, j, :, 0:64], rot[:, j, :, 64:P]
                    done(eng.tensor_tensor(lo, x1, cos, ALU.mult))
                    done(eng.tensor_tensor(rot_tmp, x2, sin, ALU.mult))
                    done(eng.tensor_tensor(lo, lo, rot_tmp, ALU.subtract))
                    done(eng.tensor_tensor(hi, x2, cos, ALU.mult))
                    done(eng.tensor_tensor(rot_tmp, x1, sin, ALU.mult))
                    done(eng.tensor_tensor(hi, hi, rot_tmp, ALU.add))
                    eng.sem_inc(sem("rot_ready"), 1)

            def store(i):
                for j in range(4):
                    eng.wait_ge(sem("y_made"), n(i, 4, j + 1))
                    row = i * (2 * P) + (j if j < 2 else 6 + j) * P
                    dst = y0_rows[row:row + P, :] if isinstance(i, int) else y0_rows[ds(row, P), :]
                    eng.dma_start(dst, gate[:, j, :]).then_inc(sem(f"y0_stored{j}"), 16)

            eng.wait_ge(sem("l0_drained"), N_HEADS)
            rotate(0)
            rotate(1)
            store(0)
            with eng.Fori(1, 3) as i:
                rotate(i + 1)
                store(i)
            store(3)

        def gates_sync(sp):
            load_chunk(sp, Chunk(N_BA), A["dn_w_in"][:, C_BA:C_BA + 64], cols=KT * 64)
            for j, col in enumerate((0, C_K1, C_V1, C_V1 + P)):
                load_chunk(sp, Chunk(N_FIRST + j), A["dn_w_in"][:, col:col + P])

        def gates_act(act):
            act.dma_start(k1, A["k1"]).then_inc(sem("head_cols_loaded"), 16)
            for j, name in enumerate(("dn_a_log", "dn_dt_bias")):
                act.dma_start(head_cols[0:H_V, j:j + 1], A[name]).then_inc(sem("head_cols_loaded"), 16)
            norm_stats_act(act, 1)
            norm_turn_act(act, 1, "dn_norm")
            c = Chunk(N_BA)
            split_hi(act, c.plus(2))
            act.wait_ge(sem("chunk_done"), c.count(1))
            act.wait_ge(sem("head_cols_loaded"), 48)
            act.activation(ba_t[0:H_V, :], bank[1][0:H_V, :], ACT.Sigmoid).then_inc(sem("softplus"), 1)
            act.activation(a_t[0:H_V, :], bank[1][H_V:2 * H_V, :], ACT.Identity,
                           bias=head_cols[0:H_V, 1:2]).then_inc(sem("softplus"), 1)
            act.activation(head_cols[0:H_V, 2:3], head_cols[0:H_V, 0:1], ACT.Exp).then_inc(
                sem("softplus"), 1)
            act.wait_ge(sem("softplus"), 2)
            act.activation(sp_1[0:H_V, :], a_t[0:H_V, :], ACT.Abs).then_inc(sem("softplus"), 1)
            act.wait_ge(sem("softplus"), 4)
            act.activation(sp_1[0:H_V, :], sp_1[0:H_V, :], ACT.Exp, scale=-1.0).then_inc(sem("softplus"), 1)
            act.wait_ge(sem("softplus"), 5)
            act.activation(sp_2[0:H_V, :], sp_1[0:H_V, :], ACT.Ln, bias=one_col[0:H_V, :]).then_inc(
                sem("softplus"), 1)
            split_hi(act, c.plus(3))
            act.wait_ge(sem("h_mid_stored"), 64)
            conv_first_tap(act, 0, 0)
            act.wait_ge(sem("gates_turned"), 1)
            act.activation(gate_tab[:, 1].rearrange("p t h -> p (t h)"), bank[3][:, 0:P], ACT.Copy).then_inc(
                sem("g_n_ready"), 1)
            act.activation(g_n.rearrange("p t h -> p (t h)"), bank[3][:, P:2 * P], ACT.Copy).then_inc(
                sem("g_n_ready"), 1)
            conv_silu(act, 0, 0)
            split_hi(act, c.plus(4))
            conv_first_tap(act, 1, 0)
            act.wait_ge(sem("gates_turned"), 2)
            act.activation(gate_tab[:, 0].rearrange("p t h -> p (t h)"), bank[2][:, 0:P], ACT.Copy).then_inc(
                sem("tab_ready"), 1)
            act.activation(gate_tab[:, 4].rearrange("p t h -> p (t h)"), bank[2][:, P:2 * P], ACT.Exp).then_inc(
                sem("tab_ready"), 1)
            act.activation(sp_3[:, P:2 * P], bank[2][:, P:2 * P], ACT.Copy).then_inc(sem("tab_ready"), 1)
            act.wait_ge(sem("tab_ready"), 1)
            act.activation(sp_3[:, 0:P], gate_tab[:, 0].rearrange("p t h -> p (t h)"), ACT.Exp).then_inc(
                sem("tab_ready"), 1)
            act.wait_ge(sem("tab_steps"), 1)
            act.activation(gate_tab[:, 3].rearrange("p t h -> p (t h)"), sp_3[:, 2 * P:3 * P],
                           ACT.Exp).then_inc(sem("tab_ready"), 1)
            act.wait_ge(sem("gates_turned"), 3)
            act.activation(a_t[0:H_V, :], bank[3][0:H_V, :], ACT.Copy).then_inc(sem("tab_ready"), 1)
            act.wait_ge(sem("tab_ready"), 6)
            act.dma_start(g_rows, a_t[0:H_V, :]).then_inc(sem("g_rows_stored"), 16)
            conv_silu(act, 1, 0)
            split_hi(act, c.plus(5))
            conv_first_tap(act, 2, 0)
            conv_silu(act, 2, 0)
            split_hi(act, c.plus(6))
            conv_first_tap(act, 3, 0)

        def gates_dve(dve):
            norm_rows_dve(dve, 1)
            norm_turn_dve(dve, 1, "dn_norm")
            split_lo(dve, Chunk(N_BA + 2))
            dve.wait_ge(sem("softplus"), 6)
            dve.scalar_tensor_tensor(out=sp_2[0:H_V, :], in0=a_t[0:H_V, :], scalar=0.0, in1=sp_2[0:H_V, :],
                                     op0=ALU.max, op1=ALU.add).then_inc(sem("g_log"), 1)
            dve.wait_ge(sem("g_log"), 1)
            dve.tensor_scalar(sp_2[0:H_V, :], sp_2[0:H_V, :], head_cols[0:H_V, 2:3], -1.0, ALU.mult,
                              ALU.mult).then_inc(sem("g_log"), 1)
            split_lo(dve, Chunk(N_BA + 3))
            conv_taps(dve, 0, 0)
            split_lo(dve, Chunk(N_BA + 4))
            conv_taps(dve, 1, 0)
            dve.wait_ge(sem("tab_ready"), 3)
            dve.tensor_tensor(sp_3[:, 2 * P:3 * P], sp_3[:, P:2 * P],
                              gate_tab[:, 0].rearrange("p t h -> p (t h)"), ALU.subtract).then_inc(
                sem("tab_steps"), 1)
            dve.wait_ge(sem("tab_ready"), 4)
            dve.tensor_scalar(gate_tab[:, 2].rearrange("p t h -> p (t h)"), sp_3[:, 0:P], -1.0, None,
                              ALU.mult).then_inc(sem("tab_steps"), 1)
            split_lo(dve, Chunk(N_BA + 5))
            conv_taps(dve, 2, 0)
            split_lo(dve, Chunk(N_BA + 6))
            conv_taps(dve, 3, 0)
            dve.wait_ge(sem("tab_ready"), 5)
            dve.wait_ge(sem("tab_steps"), 2)

        def gates_pe(pe):
            norm_pe(pe, 1)
            t_products(pe, Chunk(N_BA), width=64)
            t_products(pe, Chunk(N_FIRST))
            pe.wait_ge(sem("g_log"), 2)
            for j, src in enumerate((ba_t, sp_2)):
                for t in range(NT):
                    m = pe.transpose(bank[3][:, j * P + t * H_V:j * P + (t + 1) * H_V],
                                     src[0:H_V, ts(t, P)], ident[0:H_V, 0:H_V])
            m.then_inc(sem("gates_turned"), 1)
            t_products(pe, Chunk(N_FIRST + 1))
            pe.wait_ge(sem("g_n_ready"), 2)
            g_cols = g_n.rearrange("p t h -> p (t h)")
            pe.matmul(bank[2][:, 0:P], const("tri_up"), g_cols, start=True, stop=True)
            pe.matmul(bank[2][:, P:2 * P], ones, g_cols, start=True, stop=True).then_inc(sem("gates_turned"), 1)
            pe.wait_ge(sem("tab_ready"), 1)
            for t in range(NT):
                m = pe.transpose(bank[3][0:H_V, ts(t, P)], gate_tab[:, 0, t, :], ident)
            m.then_inc(sem("gates_turned"), 1)
            t_products(pe, Chunk(N_FIRST + 2), free=(sem("conv_drained"), 1))
            t_products(pe, Chunk(N_FIRST + 3), free=(sem("conv_drained"), 2))
            pe.wait_ge(sem("tab_ready"), 6)

        def conv_chunk(j, g):
            if isinstance(g, int) and g == 0:
                return Chunk(N_FIRST + j)
            return Chunk(N_GROUPS - 6 + 2 + j, g, 6)

        def tap_col(tap, j, g):
            a = tap * 64 + (0, 16, 32, 33)[j]
            step = (1, 1, 2, 2)[j]
            if isinstance(g, int):
                return taps[:, a + step * g:a + step * g + 1]
            return taps[:, ds(g * step + a, 1)]

        def conv_first_tap(act, j, g):
            c = conv_chunk(j, g)
            act.wait_ge(sem("chunk_done"), c.count(1))
            act.activation(cs[:, j, :], bank[c.slot][:, :], ACT.Copy, scale=tap_col(3, j, g)).then_inc(
                sem("conv_started"), 1)

        def conv_taps(dve, j, g):
            for back in (1, 2, 3):
                conv_tap(dve, j, g, back)

        def conv_tap(dve, j, g, back):
            c = conv_chunk(j, g)
            if back == 1:
                dve.wait_ge(sem("conv_started"), n(g, 4, j + 1))
            else:
                dve.wait_ge(sem("conv_tap"), n(g, 8, 2 * j + back - 1))
            dve.scalar_tensor_tensor(out=cs[:, j, back:SEQ], in0=bank[c.slot][:, 0:SEQ - back],
                                     scalar=tap_col(3 - back, j, g), in1=cs[:, j, back:SEQ],
                                     op0=ALU.mult, op1=ALU.add).then_inc(
                sem("conv_tap" if back < 3 else "conv_drained"), 1)

        def conv_silu(act, j, g):
            act.wait_ge(sem("conv_drained"), n(g, 4, j + 1))
            act.activation(cs[:, j, :], cs[:, j, :], ACT.Silu).then_inc(sem("conv_ready"), 1)
            if j < 2:
                act.wait_ge(sem("conv_ready"), n(g, 4, j + 1))
                act.activation(sq[:, j, :], cs[:, j, :], ACT.Square).then_inc(sem("sq_ready"), 1)

        WORK = ((2, 3), (4, 5))
        OUTB = (6, 7)
        GAPS = 31
        Y_FROM, Y_STEPS = 12, (17, 20, 23, 26)
        BETWEEN = 92

        def halves(t):
            return slice(t * P, t * P + P // 2), slice(t * P + P // 2, (t + 1) * P)

        def gap_at(j):
            return KT + ((BETWEEN - KT) * (j - 1)) // (GAPS - 1) if j else KT - 2

        def group_chunk(g, k):
            return Chunk(N_GROUPS + k, g, 6)

        def group_sync(sp, g, last=False):
            cols = [C_Z1, C_Z1 + P, P, C_K1 + P, C_V1 + 256, C_V1 + 384]
            per = [256, 256, 128, 128, 256, 256]
            for k in range(2 if last else 6):
                a = g * per[k] + cols[k]
                src = A["dn_w_in"][:, a:a + P] if isinstance(g, int) else A["dn_w_in"][:, ds(a, P)]
                load_chunk(sp, group_chunk(g, k), src)

        def group_pe(pe, g, last=False):
            end = 32 if last else 96
            at_k = [0]

            def products(upto):
                while at_k[0] < min(upto, end):
                    k, a = divmod(at_k[0], KT)
                    b = min(KT, a + min(upto, end) - at_k[0])
                    free = {0: (sem("conv_drained"), n(g, 4, 3)), 1: (sem("conv_drained"), n(g, 4, 4)),
                            2: (sem("z_ready"), n(g, 2, 1)), 3: (sem("z_ready"), n(g, 2, 2)),
                            4: (sem("conv_drained"), n(g, 4, 5)), 5: (sem("conv_drained"), n(g, 4, 6))}[k]
                    t_products(pe, group_chunk(g, k), a, b, free=free)
                    at_k[0] += b - a

            step = [0]

            def gap():
                step[0] += 1
                products(gap_at(step[0]))

            pe.wait_ge(sem("sq_ready"), n(g, 2, 2))
            earlier(pe, "y1_made", g, 2)
            pe.matmul(bank[4][:, :], ones, sq[:, 1, :], start=True, stop=True).then_inc(sem("ssq_done"), 1)
            pe.matmul(bank[2][:, :], ones, sq[:, 0, :], start=True, stop=True).then_inc(sem("ssq_done"), 1)
            pe.wait_ge(sem("conv_ready"), n(g, 4, 3))
            for t in range(NT):
                m = pe.transpose(bank[5][:, ts(t, P)], cs[:, 2, ts(t, P)], ident)
            m.then_inc(sem("v_turned0"), 1)
            products(8)
            pe.wait_ge(sem("kn_ready"), n(g, 1, 1))
            earlier(pe, "on_ready", g, 2)
            for t in range(NT):
                m = pe.matmul(bank[6][:, ts(t, P)], kn[:, ts(t, P)], kn[:, ts(t, P)], start=True, stop=True)
            m.then_inc(sem("kk_done"), 1)
            for t in range(NT):
                m = pe.transpose(bank[3][:, ts(t, P)], kn[:, ts(t, P)], ident)
            m.then_inc(sem("k_turned"), 1)
            pe.wait_ge(sem("qn_ready"), n(g, 1, 1))
            for t in range(NT):
                m = pe.matmul(bank[7][:, ts(t, P)], kn[:, ts(t, P)], qn[:, ts(t, P)], start=True, stop=True)
            m.then_inc(sem("kq_done"), 1)
            products(gap_at(0))
            for e in range(2):
                pe.wait_ge(sem("inv_p_ready"), n(g, 14, 2 * (1) - 1 + e))
                if e == 0:
                    pe.wait_ge(sem("k_rows_ready"), n(g, 1, 1))
                else:
                    pe.wait_ge(sem("v_n_ready0"), n(g, 1, 1))
                for t in range(NT):
                    m = pe.transpose(bank[WORK[e][1]][:, ts(t, P)], inv_p[:, e, ts(t, P)], ident)
                m.then_inc(sem("inv_turned"), 1)
            gap()
            pe.wait_ge(sem("l2_ready"), n(g, 2, 2))
            for L in range(len(LEVELS)):
                for e in range(2):
                    pe.wait_ge(sem("inv_t_ready"), n(g, 12, 2 * (L + 1) - 1 + e))
                    for t in range(NT):
                        left, right = halves(t)
                        if LEVELS[L] == P // 2:
                            m = pe.matmul(bank[WORK[e][0]][P // 2:P, left], f_up[:, e, right],
                                          inv_t[:, e, left], start=True, stop=True)
                        else:
                            m = pe.matmul(bank[WORK[e][0]][:, ts(t, P)], f_up[:, e, ts(t, P)],
                                          inv_t[:, e, ts(t, P)], start=True, stop=True)
                    m.then_inc(sem("z_done"), 1)
                gap()
                if L == 0:
                    pe.wait_ge(sem("conv_ready"), n(g, 4, 4))
                    pe.wait_ge(sem("f_ready"), n(g, 2, 2))
                    for t in range(NT):
                        m = pe.transpose(bank[6][:, ts(t, P)], cs[:, 3, ts(t, P)], ident)
                    m.then_inc(sem("v_turned1"), 1)
                for e in range(2):
                    pe.wait_ge(sem("z_m_ready"), n(g, 12, 2 * (L + 1) - 1 + e))
                    for t in range(NT):
                        left, right = halves(t)
                        if LEVELS[L] == P // 2:
                            m = pe.matmul(bank[WORK[e][1]][0:P // 2, right], z_m[:, e, left],
                                          inv_p[:, e, right], start=True, stop=True)
                        else:
                            m = pe.matmul(bank[WORK[e][1]][:, ts(t, P)], z_m[:, e, ts(t, P)],
                                          inv_p[:, e, ts(t, P)], start=True, stop=True)
                    m.then_inc(sem("zp_done"), 1)
                gap()
                if L < len(LEVELS) - 1:
                    for e in range(2):
                        pe.wait_ge(sem("inv_p_ready"), n(g, 14, 2 * (L + 2) - 1 + e))
                        for t in range(NT):
                            m = pe.transpose(bank[WORK[e][0]][:, ts(t, P)], inv_p[:, e, ts(t, P)], ident)
                        m.then_inc(sem("inv_turned"), 1)
                    gap()
            for t in range(NT):
                if t:
                    for e in range(2):
                        pe.wait_ge(sem("state_ready"), n(g, 6, 2 * (t) - 1 + e))
                        pe.matmul(bank[WORK[e][0]][:, 0:P], kn[:, ts(t, P)], state[:, e, :], start=True,
                                  stop=True).then_inc(sem("ks_done"), 1)
                        pe.matmul(bank[OUTB[e]][:, ts(t, P)], q_dec[:, e, ts(t, P)], state[:, e, :],
                                  start=True, stop=False)
                    gap()
                for e in range(2):
                    if t:
                        pe.wait_ge(sem("r_ready"), n(g, 6, 2 * (t) - 1 + e))
                    else:
                        pe.wait_ge(sem("inv_p_ready"), n(g, 14, 2 * (7) - 1 + e))
                        pe.wait_ge(sem("attn_ready"), n(g, 2, e + 1))
                        pe.wait_ge(sem("v_n_ready1"), n(g, 1, 1))
                    pe.matmul(bank[WORK[e][1]][:, 0:P], inv_p[:, e, ts(t, P)],
                              r_n[:, e, :] if t else v_n[:, e, 0, :], start=True, stop=True).then_inc(
                        sem("tr_done"), 1)
                gap()
                for e in range(2):
                    pe.wait_ge(sem("v_new_ready"), n(g, 8, 2 * (t + 1) - 1 + e))
                    if t < NT - 1:
                        if t == 0:
                            pe.wait_ge(sem("k_tail_ready"), n(g, 2, e + 1))
                            pe.wait_ge(sem("q_dec_ready"), n(g, 2, e + 1))
                            pe.wait_ge(sem("attn_ready"), n(g, 2, 2))
                        pe.matmul(bank[WORK[e][0]][:, 0:P], k_tail[:, e, t, :], v_new[:, e, :], start=True,
                                  stop=True).then_inc(sem("kv1_done"), 1)
                    m = pe.matmul(bank[OUTB[e]][:, ts(t, P)], attn_t[:, e, ts(t, P)], v_new[:, e, :],
                                  start=(t == 0), stop=True)
                    m.then_inc(sem("o_done"), 1)
                gap()
            products(96)
            if last:
                out_pe(pe, "out1a", part="start")
            for e in range(2):
                pe.wait_ge(sem("on_ready"), n(g, 2, e + 1))
                for t in range(NT):
                    m = pe.transpose(bank[WORK[e][1]][:, ts(t, P)], o_n[:, e, ts(t, P)], ident)
                m.then_inc(sem("o_turned"), 1)

        def crossing(k):
            return min(j for j in range(GAPS + 1) if gap_at(j) >= (k + 1) * KT)

        def background(j, last):
            chunks = range(2 if last else 5)
            return [(k, j - crossing(k)) for k in chunks if 0 <= j - crossing(k) < 5]

        def group_act(act, g, last=False):
            first = isinstance(g, int) and g == 0

            def stage(k, what):
                c = group_chunk(g, k)
                if what == 0 and k < 2:
                    act.wait_ge(sem("chunk_done"), c.count(1))
                    earlier(act, "y1_made", g, 2)
                    act.activation(zs[:, k, :], bank[c.slot][:, :], ACT.Silu).then_inc(sem("z_ready"), 1)
                elif what == 0:
                    if k < 4:
                        act.wait_ge(sem("kq_done"), n(g, 1, 1))
                    conv_first_tap(act, k - 2, g + 1)
                if what < 2:
                    split_hi_half(act, c.plus(2), what)
                if what == 4 and k >= 2:
                    conv_silu(act, k - 2, g + 1)

            step = [0]

            def gap():
                step[0] += 1
                for k, what in background(step[0], last):
                    stage(k, what)
                if last and step[0] == Y_FROM:
                    act.wait_ge(sem("chunk_done"), OUTS["out1a"][0])
                    for place in range(4):
                        y_load(act, "out1a", place)
                if last and step[0] in Y_STEPS:
                    y_hi(act, "out1a", Y_STEPS.index(step[0]))

            earlier(act, "qn_ready", g, 1)
            for j, b in ((1, 4), (0, 2)):
                act.wait_ge(sem("ssq_done"), n(g, 2, 2 - j))
                act.activation(rs[:, j, :], bank[b][:, :], ACT.Ln, bias=eps_col).then_inc(
                    sem("group_ln_done"), 1)
            for j in (1, 0):
                act.wait_ge(sem("group_ln_done"), n(g, 3, 2 - j))
                act.activation(rs[:, j, :], rs[:, j, :], ACT.Exp, scale=-0.5).then_inc(sem("l2_ready"), 1)
            for e in range(2):
                act.wait_ge(sem("dec_log"), n(g, 2, e + 1))
                act.activation(dec[:, e, :], dec[:, e, :], ACT.Exp).then_inc(sem("dec_ready"), 1)
            if not first:
                for half in range(2):
                    split_hi_half(act, group_chunk(g, 1), half)
                conv_first_tap(act, 3, g)
            earlier(act, "q_dec_ready", g, 2)
            for e in range(2):
                act.activation(eg[:, e, :], g_row[:, e, :], ACT.Exp).then_inc(sem("eg_ready"), 1)
            act.wait_ge(sem("v_turned0"), n(g, 1, 1))
            act.activation(v_n[:, 0], by_tile(bank[5][:, :]), ACT.Copy).then_inc(sem("v_n_ready0"), 1)
            act.wait_ge(sem("k_turned"), n(g, 1, 1))
            act.activation(k_rows, by_tile(bank[3][:, :]), ACT.Copy).then_inc(sem("k_rows_ready"), 1)
            def drain_inv(e, level):
                b = WORK[e][1] if level == 0 else WORK[e][0]
                act.wait_ge(sem("inv_turned"), n(g, 12, 2 * (level + 1) - 1 + e))
                act.activation(inv_t[:, e, :], bank[b][:, :], ACT.Copy).then_inc(sem("inv_t_ready"), 1)

            for e in range(2):
                drain_inv(e, 0)
            conv_silu(act, 3, g)
            for k, what in background(0, last):
                stage(k, what)
            gap()
            for L in range(len(LEVELS)):
                gap()
                if L == 0:
                    act.wait_ge(sem("v_turned1"), n(g, 1, 1))
                    act.activation(v_n[:, 1], by_tile(bank[6][:, :]), ACT.Copy).then_inc(
                        sem("v_n_ready1"), 1)
                gap()
                if L < len(LEVELS) - 1:
                    for e in range(2):
                        drain_inv(e, L + 1)
                    gap()
            for t in range(NT):
                if t:
                    gap()
                for e in range(2):
                    act.wait_ge(sem("tr_done"), n(g, 8, 2 * (t + 1) - 1 + e))
                    if t:
                        act.wait_ge(sem("o_done"), n(g, 8, 2 * (t) - 1 + e))
                    act.activation(v_new[:, e, :], bank[WORK[e][1]][:, 0:P], ACT.Copy,
                                   scale=gt[:, 1, t, e:e + 1]).then_inc(sem("v_new_ready"), 1)
                gap()
                gap()
            for e in range(2):
                act.wait_ge(sem("o_done"), n(g, 8, 2 * (NT) - 1 + e))
                for t in range(NT):
                    act.activation(o_n[:, e, ts(t, P)], bank[OUTB[e]][:, ts(t, P)], ACT.Square,
                                   accum_out=o_stat[:, e, 0, t:t + 1]).then_inc(sem("o_ssq"), 1)
            act.wait_ge(sem("o_ssq"), n(g, 8, 8))
            rstd(act, o_stat[:, :, 1, :], o_stat[:, :, 0, :], 1.0 / P, "group_ln_done",
                 n(g, 3, 3)).then_inc(sem("o_rstd"), 1)
            while step[0] < GAPS:
                gap()

        def group_dve(dve, g, last=False):
            first = isinstance(g, int) and g == 0

            def stage(k, what):
                if 1 <= what <= 3 and k >= 2:
                    conv_tap(dve, k - 2, g + 1, what)
                if 2 <= what <= 3:
                    split_lo_half(dve, group_chunk(g, k + 2), what - 2)

            step = [0]

            def gap():
                step[0] += 1
                for k, what in background(step[0], last):
                    stage(k, what)
                if last and step[0] - 1 in Y_STEPS:
                    y_lo(dve, "out1a", Y_STEPS.index(step[0] - 1))

            cols = gate_tab[:, :, :, 2 * g:2 * g + 2] if isinstance(g, int) else \
                gate_tab[:, :, :, ds(g * 2, 2)]
            flat = "p k t h -> p (k t) h"
            earlier(dve, "k_tail_ready", g, 2)
            dve.tensor_copy(gt.rearrange(flat), cols.rearrange(flat)).then_inc(sem("gt_ready"), 1)
            dve.wait_ge(sem("gt_ready"), n(g, 1, 1))
            dve.wait_ge(sem("g_row_loaded"), n(g, 16, 16))
            for e in range(2):
                for t in range(NT):
                    m = dve.scalar_tensor_tensor(out=dec[:, e, ts(t, P)], in0=g_row[:, e, ts(t, P)],
                                                 scalar=gt[:, 0, t, e:e + 1], in1=k1c("hide_up"),
                                                 op0=ALU.subtract, op1=ALU.add)
                m.then_inc(sem("dec_log"), 1)
            dve.wait_ge(sem("l2_ready"), n(g, 2, 1))
            dve.tensor_tensor(kn, cs[:, 1, :], rs[:, 1, :], ALU.mult).then_inc(sem("kn_ready"), 1)
            dve.wait_ge(sem("l2_ready"), n(g, 2, 2))
            dve.scalar_tensor_tensor(out=qn, in0=cs[:, 0, :], scalar=P ** -0.5, in1=rs[:, 0, :],
                                     op0=ALU.mult, op1=ALU.mult).then_inc(sem("qn_ready"), 1)
            for e in range(2):
                dve.wait_ge(sem("kk_done"), n(g, 1, 1))
                dve.wait_ge(sem("dec_ready"), n(g, 2, e + 1))
                for t in range(NT):
                    m = dve.scalar_tensor_tensor(out=f_up[:, e, ts(t, P)], in0=bank[6][:, ts(t, P)],
                                                 scalar=gt[:, 1, t, e:e + 1], in1=dec[:, e, ts(t, P)],
                                                 op0=ALU.mult, op1=ALU.mult)
                m.then_inc(sem("f_ready"), 1)
                dve.wait_ge(sem("f_ready"), n(g, 2, e + 1))
                dve.tensor_tensor(by_tile(inv_p[:, e, :]), by_tile(f_up[:, e, :]), tiled(k1c("pair_up")),
                                  ALU.mult).then_inc(sem("pair_ready"), 1)
                dve.wait_ge(sem("pair_ready"), n(g, 2, e + 1))
                dve.tensor_tensor(by_tile(inv_p[:, e, :]), tiled(ident), by_tile(inv_p[:, e, :]),
                                  ALU.subtract).then_inc(sem("inv_p_ready"), 1)
            if not first:
                split_lo(dve, group_chunk(g, 1))
            if not first:
                conv_taps(dve, 3, g)
            gap()
            for L in range(len(LEVELS)):
                for e in range(2):
                    dve.wait_ge(sem("z_done"), n(g, 12, 2 * (L + 1) - 1 + e))
                    w = P // 2 if LEVELS[L] == P // 2 else P
                    dve.tensor_tensor(by_tile(z_m[:, e, :])[:, :, 0:w],
                                      by_tile(bank[WORK[e][0]][:, :])[:, :, 0:w],
                                      tiled(k1c("levels")[:, ts(L, P)])[:, :, 0:w], ALU.mult).then_inc(
                        sem("z_m_ready"), 1)
                gap()
                if L == 0:
                    for e in range(2):
                        dve.wait_ge(sem("kq_done"), n(g, 1, 1))
                        dve.tensor_tensor(attn_t[:, e, :], bank[7][:, :], dec[:, e, :],
                                          ALU.mult).then_inc(sem("attn_ready"), 1)
                for e in range(2):
                    dve.wait_ge(sem("zp_done"), n(g, 12, 2 * (L + 1) - 1 + e))
                    n_rows, first_col = (P // 2, P // 2) if LEVELS[L] == P // 2 else (P, 0)
                    changed = by_tile(inv_p[:, e, :])[0:n_rows, :, first_col:P]
                    dve.tensor_tensor(changed, changed,
                                      by_tile(bank[WORK[e][1]][:, :])[0:n_rows, :, first_col:P],
                                      ALU.subtract).then_inc(sem("inv_p_ready"), 1)
                gap()
                if L < len(LEVELS) - 1:
                    gap()
            for t in range(NT):
                if t:
                    for e in range(2):
                        dve.wait_ge(sem("ks_done"), n(g, 6, 2 * (t) - 1 + e))
                        dve.scalar_tensor_tensor(out=r_n[:, e, :], in0=bank[WORK[e][0]][:, 0:P],
                                                 scalar=gt[:, 2, t, e:e + 1], in1=v_n[:, e, t, :],
                                                 op0=ALU.mult, op1=ALU.add).then_inc(sem("r_ready"), 1)
                    gap()
                gap()
                if t < NT - 1:
                    for e in range(2):
                        dve.wait_ge(sem("kv1_done"), n(g, 6, 2 * (t + 1) - 1 + e))
                        if t == 0:
                            m = dve.tensor_copy(state[:, e, :], bank[WORK[e][0]][:, 0:P])
                        else:
                            m = dve.scalar_tensor_tensor(out=state[:, e, :], in0=state[:, e, :],
                                                         scalar=gt[:, 4, t, e:e + 1],
                                                         in1=bank[WORK[e][0]][:, 0:P], op0=ALU.mult,
                                                         op1=ALU.add)
                        m.then_inc(sem("state_ready"), 1)
                gap()
            dve.wait_ge(sem("o_rstd"), n(g, 1, 1))
            for e in range(2):
                dve.tensor_tensor(by_tile(o_n[:, e, :]), by_tile(bank[OUTB[e]][:, :]),
                                  spread(o_stat[:, e, 1, :]), ALU.mult).then_inc(sem("on_ready"), 1)
            while step[0] < GAPS:
                gap()
            dve.wait_ge(sem("z_ready"), n(g, 2, 2))
            for e in range(2):
                dve.wait_ge(sem("o_turned"), n(g, 2, e + 1))
                earlier(dve, f"y1_stored{e}", g, 16)
                dve.scalar_tensor_tensor(out=y_out[:, e, :], in0=bank[WORK[e][1]][:, :],
                                         scalar=vcol("dn_out_norm"), in1=zs[:, e, :], op0=ALU.mult,
                                         op1=ALU.mult).then_inc(sem("y1_made"), 1)

        def g_row_load(eng, g):
            src = g_rows[2 * g:2 * g + 2, :] if isinstance(g, int) else g_rows[ds(g * 2, 2), :]
            eng.dma_start(g_row, src.rearrange("(o h) s -> o h s", o=1).broadcast_to([P, 2, SEQ])).then_inc(
                sem("g_row_loaded"), 16)

        def group_pool(eng, g, last=False):
            for e in range(2):
                eng.wait_ge(sem("eg_ready"), n(g, 2, e + 1))
                eng.wait_ge(sem("qn_ready"), n(g, 1, 1))
                eng.tensor_tensor(q_dec[:, e, :], qn, eg[:, e, :], ALU.mult).then_inc(sem("q_dec_ready"), 1)
            eng.wait_ge(sem("k_rows_ready"), n(g, 1, 1))
            eng.wait_ge(sem("gt_ready"), n(g, 1, 1))
            for e in range(2):
                eng.tensor_tensor(k_tail[:, e], k_rows, spread(gt[:, 3, :, e]), ALU.mult).then_inc(
                    sem("k_tail_ready"), 1)
            if not last:
                g_row_load(eng, g + 1)
            for e in range(2):
                eng.wait_ge(sem("y1_made"), n(g, 2, e + 1))
                row = g * (2 * P) + e * P
                dst = y1_rows[row:row + P, :] if isinstance(g, int) else y1_rows[ds(row, P), :]
                eng.dma_start(dst, y_out[:, e, :]).then_inc(sem(f"y1_stored{e}"), 16)

        block = ctx.enter_context(nc.Block())

        @block.sync
        def _(sp):
            pre_sync(sp)
            heads_sync(sp)
            out_sync(sp, "out0")
            gates_sync(sp)
            group_sync(sp, 0)
            with sp.Fori(1, H_QK - 1) as g:
                group_sync(sp, g)
            group_sync(sp, H_QK - 1, last=True)
            out_sync(sp, "out1a")
            out_sync(sp, "out1b")
            sp.wait_ge(sem("out_stored"), 16 * (3 + NT))

        @block.gpsimd
        def _(eng):
            heads_pool(eng)
            for j in range(4):
                eng.wait_ge(sem(f"y0_stored{j}"), 64)
            out_pool(eng, "out0")
            eng.wait_ge(sem("h_mid_stored"), 64)
            eng.wait_ge(sem("g_rows_stored"), 16)
            g_row_load(eng, 0)
            group_pool(eng, 0)
            with eng.Fori(1, H_QK - 1) as g:
                group_pool(eng, g)
            group_pool(eng, H_QK - 1, last=True)
            for e in range(2):
                eng.wait_ge(sem(f"y1_stored{e}"), 16 * H_QK)
            out_pool(eng, "out1a")
            out_pool(eng, "out1b")

        @block.scalar
        def _(act):
            pre_act(act)
            heads_act(act)
            out_act(act, "out0")
            gates_act(act)
            group_act(act, 0)
            with act.Fori(1, H_QK - 1) as g:
                group_act(act, g)
            group_act(act, H_QK - 1, last=True)
            out_act(act, "out1a")
            out_act(act, "out1b")

        @block.vector
        def _(dve):
            pre_dve(dve)
            heads_dve(dve)
            out_dve(dve, "out0")
            gates_dve(dve)
            group_dve(dve, 0)
            with dve.Fori(1, H_QK - 1) as g:
                group_dve(dve, g)
            group_dve(dve, H_QK - 1, last=True)
            out_dve(dve, "out1a")
            out_dve(dve, "out1b")

        @block.tensor
        def _(pe):
            pre_pe(pe)
            heads_pe(pe)
            pe.wait_ge(sem("l0_drained"), N_OUT0)
            out_pe(pe, "out0")
            gates_pe(pe)
            group_pe(pe, 0)
            with pe.Fori(1, H_QK - 1) as g:
                group_pe(pe, g)
            group_pe(pe, H_QK - 1, last=True)
            out_pe(pe, "out1a", part="rest")
            out_pe(pe, "out1b")


_SHAPES = {"x": (SEQ, DM), "ab_norm": (16, P), "ab_w_in": None, "ab_kv_norm": (2, P), "ab_w_uk": None,
           "ab_w_uv": (H_A * D_C, P), "ab_q_norm": (1, P), "ab_k_norm": (1, P), "ab_ret_norm": (8, P),
           "ab_w_out": None, "dn_norm": (16, P), "dn_w_in": None, "dn_conv": (256, P),
           "dn_a_log": (H_V, 1), "dn_dt_bias": (H_V, 1), "dn_out_norm": (1, P), "dn_w_out": None}


def kernel(**inputs):
    import concourse.bacc as bacc
    from concourse.bass_utils import run_bass_kernel_spmd

    nc = bacc.Bacc("TRN2", target_bir_lowering=False, num_devices=1)
    arrays, aps = {}, {}
    for name, shape in _SHAPES.items():
        a = np.asarray(inputs[name])
        arrays[name] = np.ascontiguousarray(a.reshape(shape or a.shape[1:]))
    arrays["k0"], arrays["k1"] = constant_tables()
    for name, a in arrays.items():
        aps[name] = nc.dram_tensor(name, a.shape, F32, kind="ExternalInput").ap()
    aps["out"] = nc.dram_tensor("out", (SEQ, DM), F32, kind="ExternalOutput").ap()
    build(nc, aps)
    r = run_bass_kernel_spmd(nc, [arrays], core_ids=[0])
    return r.results[0]["out"].reshape(1, SEQ, DM)
```
